# Optimizing a Trainium2 kernel written in Bass

```python
import jax, jax.numpy as jnp
from jax import lax
import numpy as np

D_MODEL = 1024
BATCH = 1
SEQ = 256
DEPTH = 2

GRID_W = 64
NA_HEADS = 8
NA_HEAD_DIM = 64
NA_WIDTH = NA_HEADS * NA_HEAD_DIM
NA_KH_MAX = 8
NA_KW = 16
FN_GROUPS = 8
FN_GROUP_DIM = 64
FN_WIDTH = FN_GROUPS * FN_GROUP_DIM
LRU_BLOCKS = 8
LRU_BLOCK_DIM = 64
LRU_WIDTH = LRU_BLOCKS * LRU_BLOCK_DIM
LRU_C = 8.0
CONV_W = 4
CONV_PAD_LEFT = 2
N_BRANCH = 3
BRANCH_WIDTH = 512
SPLITS = [NA_WIDTH, 2 * NA_WIDTH, 3 * NA_WIDTH, 3 * NA_WIDTH + FN_WIDTH,
          3 * NA_WIDTH + FN_WIDTH + LRU_WIDTH, 3 * NA_WIDTH + FN_WIDTH + 2 * LRU_WIDTH]
IN_COLS = 3 * NA_WIDTH + FN_WIDTH + 2 * LRU_WIDTH + N_BRANCH * D_MODEL
D_FF = 3 * D_MODEL
N_EXPERTS = 8
TOP_K = 2
D_FF_EXPERT = D_FF // TOP_K
N_DENSE = (DEPTH + 1) // 2
N_MOE = DEPTH // 2
RMS_EPS = 1e-6

kernel_name = 'hybrid_na_fnet_rglru_moe_encoder'

def rms_norm(x, g):
    xf = x.astype(jnp.float32)
    y = xf * lax.rsqrt(jnp.mean(xf * xf, axis=-1, keepdims=True) + RMS_EPS)
    return (y * g.astype(jnp.float32)).astype(x.dtype)

def neighbourhood_attention(q, k, v, rpb, rows):
    b, s, _ = q.shape
    kh = min(NA_KH_MAX, rows)

    def to_grid(t):
        return t.reshape(b, rows, GRID_W, NA_HEADS, NA_HEAD_DIM).transpose(0, 3, 1, 2, 4)

    qg, kg, vg = to_grid(q), to_grid(k), to_grid(v)
    cols = np.arange(GRID_W)
    col_start = np.clip(cols - NA_KW // 2, 0, GRID_W - NA_KW)
    col_idx = col_start[:, None] + np.arange(NA_KW)[None, :]
    col_off = col_idx - cols[:, None] + (NA_KW - 1)
    rpb_c = rpb.astype(jnp.float32)[:, :, col_off]
    scale = NA_HEAD_DIM ** -0.5

    def one_row(r):
        rs = jnp.clip(r - kh // 2, 0, rows - kh)
        k_band = lax.dynamic_slice_in_dim(kg, rs, kh, axis=2)
        v_band = lax.dynamic_slice_in_dim(vg, rs, kh, axis=2)
        q_row = lax.dynamic_index_in_dim(qg, r, axis=2, keepdims=False)
        k_win = k_band[:, :, :, col_idx, :]
        v_win = v_band[:, :, :, col_idx, :]
        row_off = rs + jnp.arange(kh) - r + (NA_KH_MAX - 1)
        bias = jnp.take(rpb_c, row_off, axis=1).transpose(0, 2, 1, 3)
        scores = jnp.einsum('bhcd,bhicjd->bhcij', q_row, k_win,
                            preferred_element_type=jnp.float32) * scale + bias[None]
        p = jax.nn.softmax(scores.reshape(b, NA_HEADS, GRID_W, kh * NA_KW), axis=-1)
        p = p.reshape(scores.shape).astype(v.dtype)
        return jnp.einsum('bhcij,bhicjd->bhcd', p, v_win)

    out = lax.map(one_row, jnp.arange(rows))
    return out.transpose(1, 0, 3, 2, 4).reshape(b, s, NA_WIDTH)

def fourier_mix(u):
    b, s, _ = u.shape
    ug = u.astype(jnp.float32).reshape(b, s, FN_GROUPS, FN_GROUP_DIM)
    f = jnp.fft.fft2(ug, axes=(1, 3), norm='ortho').real
    return f.reshape(b, s, FN_WIDTH).astype(u.dtype)

def centred_depthwise_conv(u, w, bias):
    s = u.shape[1]
    up = jnp.pad(u, ((0, 0), (CONV_PAD_LEFT, CONV_W - 1 - CONV_PAD_LEFT), (0, 0)))
    y = up[:, 0:s] * w[0]
    for t in range(1, CONV_W):
        y = y + up[:, t:t + s] * w[t]
    return y + bias

def block_diag(u, w, bias):
    b, s, _ = u.shape
    ub = u.reshape(b, s, LRU_BLOCKS, LRU_BLOCK_DIM)
    return jnp.einsum('bsnc,ncd->bsnd', ub, w).reshape(b, s, LRU_WIDTH) + bias

def rg_lru_direction(u, wa, ba, wx, bx, lam, reverse):
    s = u.shape[1]
    uf = u.astype(jnp.float32)
    r = jax.nn.sigmoid(block_diag(u, wa, ba).astype(jnp.float32))
    i = jax.nn.sigmoid(block_diag(u, wx, bx).astype(jnp.float32))
    log_a = -LRU_C * r * jax.nn.softplus(-lam.astype(jnp.float32))
    a = jnp.exp(log_a)
    mult = jnp.sqrt(-jnp.expm1(2.0 * log_a))
    first = s - 1 if reverse else 0
    mult = jnp.where((jnp.arange(s) == first)[None, :, None], jnp.ones_like(mult), mult)
    bterm = mult * i * uf

    def combine(c1, c2):
        a1, b1 = c1
        a2, b2 = c2
        return a1 * a2, a2 * b1 + b2

    _, h = lax.associative_scan(combine, (a, bterm), axis=1, reverse=reverse)
    return h

def recurrent_branch(u_x, u_gate, conv_w, conv_b, wa, ba, wx, bx, lam):
    c = centred_depthwise_conv(u_x, conv_w, conv_b)
    h = (rg_lru_direction(c, wa[0], ba[0], wx[0], bx[0], lam[0], False)
         + rg_lru_direction(c, wa[1], ba[1], wx[1], bx[1], lam[1], True))
    return (h * jax.nn.gelu(u_gate.astype(jnp.float32))).astype(u_x.dtype)

def hybrid_mixer(xn, rows, w_in, b_in, rpb, conv_w, conv_b, wa, ba, wx, bx, lam, w_branch, w_out):
    b, s, d = xn.shape
    proj = xn @ w_in + b_in
    q, k, v, u_f, u_x, u_g, gates = jnp.split(proj, SPLITS, axis=-1)
    y_a = neighbourhood_attention(q, k, v, rpb, rows)
    y_b = fourier_mix(u_f)
    y_c = recurrent_branch(u_x, u_g, conv_w, conv_b, wa, ba, wx, bx, lam)
    br = jnp.stack([y_a, y_b, y_c], axis=2)
    y_br = jnp.einsum('bskc,kcd->bskd', br, w_branch)
    g = jax.nn.sigmoid(gates.astype(jnp.float32)).reshape(b, s, N_BRANCH, d)
    merged = jnp.sum(g * y_br.astype(jnp.float32), axis=2).astype(xn.dtype)
    return merged @ w_out

def swiglu(x, w_gu, w_down):
    g, u = jnp.split(x @ w_gu, 2, axis=-1)
    return (jax.nn.silu(g) * u) @ w_down

def moe_swiglu(x, w_router, w_gu, w_down):
    b, s, d = x.shape
    xt = x.reshape(b * s, d)
    logits = (xt @ w_router).astype(jnp.float32)
    top_v, top_i = lax.top_k(logits, TOP_K)
    top_w = jax.nn.softmax(top_v, axis=-1)
    comb = jnp.sum(jax.nn.one_hot(top_i, N_EXPERTS, dtype=jnp.float32) * top_w[..., None], axis=1)
    y = jnp.zeros((b * s, d), jnp.float32)
    for e in range(N_EXPERTS):
        y = y + comb[:, e:e + 1] * swiglu(xt, w_gu[e], w_down[e]).astype(jnp.float32)
    return y.astype(x.dtype).reshape(b, s, d)

def setup_inputs(seed: int = 0) -> dict:
    key = jax.random.key(seed)
    ks = jax.random.split(key, 24)
    f32 = jnp.float32

    def nrm(kk, shape, scale):
        return jax.random.normal(kk, shape, f32) * scale

    a_c = jax.random.uniform(ks[11], (DEPTH, 2, LRU_WIDTH), f32, 0.9, 0.999)
    a_base = a_c ** (1.0 / LRU_C)
    lru_lambda = jnp.log(a_base) - jnp.log1p(-a_base)
    return {
        'x': nrm(ks[0], (BATCH, SEQ, D_MODEL), 1.0),
        'norm_mix_g': 1.0 + nrm(ks[1], (DEPTH, D_MODEL), 0.02),
        'w_in': nrm(ks[2], (DEPTH, D_MODEL, IN_COLS), D_MODEL ** -0.5),
        'b_in': nrm(ks[3], (DEPTH, IN_COLS), 0.02),
        'na_rpb': nrm(ks[4], (DEPTH, NA_HEADS, 2 * NA_KH_MAX - 1, 2 * NA_KW - 1), 0.02),
        'conv_w': nrm(ks[5], (DEPTH, CONV_W, LRU_WIDTH), CONV_W ** -0.5),
        'conv_b': nrm(ks[6], (DEPTH, LRU_WIDTH), 0.02),
        'lru_wa': nrm(ks[7], (DEPTH, 2, LRU_BLOCKS, LRU_BLOCK_DIM, LRU_BLOCK_DIM), LRU_BLOCK_DIM ** -0.5),
        'lru_ba': nrm(ks[8], (DEPTH, 2, LRU_WIDTH), 0.02),
        'lru_wx': nrm(ks[9], (DEPTH, 2, LRU_BLOCKS, LRU_BLOCK_DIM, LRU_BLOCK_DIM), LRU_BLOCK_DIM ** -0.5),
        'lru_bx': nrm(ks[10], (DEPTH, 2, LRU_WIDTH), 0.02),
        'lru_lambda': lru_lambda,
        'w_branch': nrm(ks[12], (DEPTH, N_BRANCH, BRANCH_WIDTH, D_MODEL), BRANCH_WIDTH ** -0.5),
        'w_out': nrm(ks[13], (DEPTH, D_MODEL, D_MODEL), D_MODEL ** -0.5),
        'norm_ffn_g': 1.0 + nrm(ks[14], (DEPTH, D_MODEL), 0.02),
        'ffn_w_gu': nrm(ks[15], (N_DENSE, D_MODEL, 2 * D_FF), D_MODEL ** -0.5),
        'ffn_w_down': nrm(ks[16], (N_DENSE, D_FF, D_MODEL), D_FF ** -0.5),
        'router_w': nrm(ks[17], (N_MOE, D_MODEL, N_EXPERTS), D_MODEL ** -0.5),
        'moe_w_gu': nrm(ks[18], (N_MOE, N_EXPERTS, D_MODEL, 2 * D_FF_EXPERT), D_MODEL ** -0.5),
        'moe_w_down': nrm(ks[19], (N_MOE, N_EXPERTS, D_FF_EXPERT, D_MODEL), D_FF_EXPERT ** -0.5),
        'final_g': 1.0 + nrm(ks[20], (D_MODEL,), 0.02),
    }

def reference(x, norm_mix_g, w_in, b_in, na_rpb, conv_w, conv_b, lru_wa, lru_ba, lru_wx, lru_bx,
              lru_lambda, w_branch, w_out, norm_ffn_g, ffn_w_gu, ffn_w_down, router_w, moe_w_gu,
              moe_w_down, final_g):
    rows = x.shape[1] // GRID_W
    h = x
    for l in range(DEPTH):
        xn = rms_norm(h, norm_mix_g[l])
        h = h + hybrid_mixer(xn, rows, w_in[l], b_in[l], na_rpb[l], conv_w[l], conv_b[l],
                             lru_wa[l], lru_ba[l], lru_wx[l], lru_bx[l], lru_lambda[l],
                             w_branch[l], w_out[l])
        xn = rms_norm(h, norm_ffn_g[l])
        if l % 2 == 0:
            h = h + swiglu(xn, ffn_w_gu[l // 2], ffn_w_down[l // 2])
        else:
            h = h + moe_swiglu(xn, router_w[l // 2], moe_w_gu[l // 2], moe_w_down[l // 2])
    return rms_norm(h, final_g)


_drawn_inputs = setup_inputs


def setup_inputs(seed=0):
    import zlib

    import numpy as np

    out = dict(_drawn_inputs(seed))
    spreads = {}
    factors = {'na_rpb': 14.599, 'lru_ba': 26.001, 'lru_bx': 7.631, 'final_g': 8.692}
    for name, (base, spread) in spreads.items():
        noise = np.random.default_rng([zlib.crc32(name.encode()), seed]).standard_normal(out[name].shape)
        drawn = base * np.exp(spread * noise) if base else spread * noise
        out[name] = __import__('jax').numpy.asarray(drawn.astype(out[name].dtype))
    for name, factor in factors.items():
        out[name] = (out[name] * factor).astype(out[name].dtype)
    return out
```

```python
import math
from contextlib import ExitStack

import numpy as np

import concourse.bass as bass
from concourse import mybir

F32 = mybir.dt.float32
F32R = mybir.dt.float32r
U32 = mybir.dt.uint32
I32 = mybir.dt.int32
ALU = mybir.AluOpType
ACT = mybir.ActivationFunctionType
AX_X = mybir.AxisListType.X
GELU_C = math.sqrt(2 / math.pi)

P = 128
SEQ, D = 256, 1024
TT = SEQ // P
KC = D // P
GRID_W = 64
ROWS = SEQ // GRID_W
HEADS, HD = 8, 64
KH_MAX, KW = 8, 16
BR = 512
BC = BR // P
IN_COLS = 3 * BR + BR + 2 * BR + 3 * D
D_FF = 3 * D
E, FE = 8, D_FF // 2
SCALE = HD ** -0.5
EPS = 1e-6
NEG = -1e30
BT_SLOTS = ROWS + 2

UNIT = 1024
RAW = 6
RAW_MOE = 18
RH = 4
CUT, CUT_MOE = 512, 704
AHEAD = RH - 1

UF, UX, Q, K, V, UG = 3, 4, 0, 1, 2, 5
GROUPS = [UF, UX, Q, K, V, UG] + list(range(6, 12))
GATE0 = 6
U_IN = 4 * len(GROUPS)
BRANCHES = [(dg, k) for dg in range(2) for k in (1, 2, 0)]
U_BR = 2 * len(BRANCHES)
U_OUT = KC
U_MIX = U_IN + U_BR + U_OUT
FF_STEPS = D_FF // 512
U_FF = 12 * FF_STEPS
FE_STEPS = FE // 512
U_EX = 12 * FE_STEPS
BASE_MIX = [0, U_MIX + U_FF]
BASE_FF = U_MIX
BASE_MOE = 2 * U_MIX + U_FF

AT_F1, AT_F2, AT_LF, AT_LB, AT_ATT = 8, 12, 16, 24, 26
AT_CONV = 9
AT_MASK = (14, 16, 18, 20)
UNITS_ATT = [(hp, t, hh) for hp in range(HEADS // 2) for t in range(TT) for hh in range(2)]
NA = len(UNITS_ATT)

C_ID, C_TRI, C_ONE, C_IOTA, C_CC, C_MASK, C_DFT, C_I8 = 0, 128, 256, 384, 640, 896, 960, 1984
C_COLS = 1992
FIRST_SLOTS = 128


def constants():
    c = np.zeros((P, C_COLS), np.float32)
    i = np.arange(P)
    c[:, C_ID:C_ID + P] = np.eye(P)
    c[:, C_TRI:C_TRI + P] = i[:, None] < i[None, :]
    c[:, C_ONE:C_ONE + P] = 1.0
    c[:, C_IOTA:C_IOTA + P] = np.where(i < FIRST_SLOTS, i, -1)
    c[:, C_IOTA + P:C_IOTA + 2 * P] = FIRST_SLOTS + i
    ang = 2 * np.pi * ((i[:, None] * i[None, :]) % HD) / HD
    same = (i[:, None] // HD) == (i[None, :] // HD)
    c[:, C_CC:C_CC + P] = np.cos(ang) * same
    c[:, C_CC + P:C_CC + 2 * P] = -np.sin(ang) * same
    col = i % GRID_W
    start = np.clip(col - KW // 2, 0, GRID_W - KW)
    kc = GRID_W - 1 - np.arange(GRID_W)
    inside = (kc[None, :] >= start[:, None]) & (kc[None, :] < start[:, None] + KW)
    c[:, C_MASK:C_MASK + GRID_W] = np.where(inside, 0.0, NEG)
    s = np.arange(SEQ)
    for t in range(TT):
        a = 2 * np.pi * (((t * P + i)[:, None] * s[None, :]) % SEQ) / SEQ
        at = C_DFT + t * 2 * SEQ
        c[:, at:at + SEQ] = np.cos(a) / math.sqrt(SEQ * HD)
        c[:, at + SEQ:at + 2 * SEQ] = np.sin(a) / math.sqrt(SEQ * HD)
    c[:, C_I8:C_I8 + 8] = np.arange(8)
    return c


def build(nc, x, norm_mix_g, w_in, b_in, rpb, conv_w, conv_b, lru_wa, lru_ba, lru_wx, lru_bx,
          lru_lambda, w_branch, w_out, norm_ffn_g, ffn_w_gu, ffn_w_down, router_w, moe_w_gu,
          moe_w_down, final_g, consts, out):
    with ExitStack() as ctx:
        def sb(name, shape, dt=F32):
            return ctx.enter_context(nc.sbuf_tensor(name, shape, dt))

        def sem(name):
            return ctx.enter_context(nc.semaphore(name))

        raw = sb("raw", [P, RAW, UNIT])
        w_hi = sb("w_hi", [P, RH, UNIT], F32R)
        w_lo = sb("w_lo", [P, RH, UNIT], F32R)
        h = sb("h", [P, TT, D])
        xh = sb("xh", [P, KC, SEQ], F32R)
        xl = sb("xl", [P, KC, SEQ], F32R)
        yh = sb("yh", [P, 3 * BC, SEQ], F32R)
        yl = sb("yl", [P, 3 * BC, SEQ], F32R)
        gates = sb("gates", [P, 3 * KC, SEQ])
        gflat = gates[:, :, :].rearrange("p c s -> p (c s)")
        hn = gflat[:, 0:TT * D].rearrange("p (t d) -> p t d", t=TT)
        junk = gflat[:, TT * D:2 * TT * D].rearrange("p (t d) -> p t d", t=TT)
        rows_in = gflat[:, 5 * D:5 * D + 2 * P].rearrange("p (a b) -> p a b", a=2)
        xrow = gflat[:, 2 * D:3 * D]
        xt_full = gflat[:, 4 * D:6 * D]
        silu_t = gflat[:, 3 * D:4 * D]
        prod_t = gflat[:, 4 * D:5 * D]
        W = BC * SEQ
        N_BIAS, N_UX = HEADS * BT_SLOTS * GRID_W, BC * (SEQ + 4)
        mix = sb("mix", [P, N_BIAS + 9 * W + N_UX])
        bias_t = mix[:, 0:N_BIAS].rearrange("p (s c) -> p s c", c=GRID_W)
        q_t, k_t, v_t, uf_t, ug_t, conv_t = (mix[:, N_BIAS + W * i:N_BIAS + W * i + W] for i in range(6))
        q_t, k_t, conv_t = (a.rearrange("p (c s) -> p c s", c=BC) for a in (q_t, k_t, conv_t))
        v_t = v_t.rearrange("p (t n) -> p t n", t=TT)
        lru = mix[:, N_BIAS + 6 * W:N_BIAS + 9 * W].rearrange("p (a n) -> p a n", a=3)
        ux_t = mix[:, N_BIAS + 9 * W:N_BIAS + 9 * W + N_UX].rearrange("p (c s) -> p c s", c=BC)
        row = sb("row", [P, D])
        p_t = sb("p_t", [P, 2, SEQ])
        pt_t = sb("pt_t", [P, 2, SEQ])
        cst = sb("cst", [P, C_COLS])
        col = sb("col", [P, 192])
        col2 = sb("col2", [P, 120])
        small = sb("small", [P, 192])
        wlru = sb("wlru", [P, 2, 2, BC, HD])
        rw = sb("rw", [P, KC, E])
        g_t = sb("g_t", [P, TT, P], F32R)
        gt_t = sb("gt_t", [P, TT, P], F32R)
        idx = sb("idx", [P, TT, 8], U32)
        cnt_i = sb("cnt_i", [P, 2], I32)
        eps_t = sb("eps_t", [P, 1])
        ps = ctx.enter_context(nc.psum_tensor("ps", [P, 8, 512], F32))

        ux_in = ux_t[:, :, 2:2 + SEQ]
        cflat = conv_t[:, :, :].rearrange("p c s -> p (c s)")
        ident = cst[:, C_ID:C_ID + P]
        tri = cst[:, C_TRI:C_TRI + P]
        ones = cst[:, C_ONE:C_ONE + P]
        NB = IN_COLS // P
        O_CW = 2 * NB
        O_CB = O_CW + 2 * 4 * BC
        O_BA = O_CB + 2 * BC
        O_BX = O_BA + 4 * BC
        O_LAM = O_BX + 4 * BC
        N_COL = O_LAM + 4 * BC
        O_SP, O_NSP, O_HBA, O_HBX, O_BQ, O_GB = 0, 16, 32, 48, 64, 72
        lam_w = small[:, 96:192].rearrange("p (a b) -> p a b", a=6)
        ss, rms, rinv = small[:, 0:2], small[:, 2:4], small[:, 4:6]
        table_in = small[:, 6:7]
        smax, nmax, rsum, rrec = small[:, 8:10], small[:, 10:12], small[:, 12:14], small[:, 14:16]
        logit = small[:, 16:32].rearrange("p (t e) -> p t e", t=TT)
        top8 = small[:, 32:48].rearrange("p (t e) -> p t e", t=TT)
        oh1 = small[:, 48:64].rearrange("p (t e) -> p t e", t=TT)
        oh2 = small[:, 64:80].rearrange("p (t e) -> p t e", t=TT)
        mask = small[:, 80:104].rearrange("p (t e) -> p t e", t=TT)
        comb = small[:, 104:128].rearrange("p (t e) -> p t e", t=TT)
        pos = small[:, 128:152].rearrange("p (t e) -> p t e", t=TT)
        wtop = small[:, 152:168].rearrange("p (t e) -> p t e", t=TT)
        cnt = small[:, 168:176]
        cmax = small[:, 176:177]
        slot_w = small[:, 177:178]
        idxf = small[:, 180:184].rearrange("p (t e) -> p t e", t=TT)
        xg_h = xh[:, 0:4, :].rearrange("p c s -> p (c s)")
        xg_l = xl[:, 0:4, :].rearrange("p c s -> p (c s)")
        ys_h = xh[:, 4:8, :].rearrange("p c s -> p (c s)")
        ys_l = xl[:, 4:8, :].rearrange("p c s -> p (c s)")
        yhf = yh[:, :, :].rearrange("p c s -> p (c s)")
        ylf = yl[:, :, :].rearrange("p c s -> p (c s)")
        xhf = xh[:, :, :].rearrange("p c s -> p (c s)")
        xlf = xl[:, :, :].rearrange("p c s -> p (c s)")

        raw_full = [sem(f"raw_full{i}") for i in range(RAW)]
        mix_full = [sem(f"mix_full{i}") for i in range(RAW_MOE - RAW)]
        hi_done, lo_dve, lo_pool, unit_used = sem("hi_done"), sem("lo_dve"), sem("lo_pool"), sem("unit_used")
        ident_in, const_in, vec_in, rw_in = sem("ident_in"), sem("const_in"), sem("vec_in"), sem("rw_in")
        x_in = [sem(f"x_in{t}") for t in range(TT)]
        bias_in, wlru_in, row_in = sem("bias_in"), sem("wlru_in"), sem("row_in")
        vec_t, col_ok, lam_act, col2_ok, zeroed = sem("vec_t"), sem("col_ok"), sem("lam_act"), sem("col2_ok"), sem("zeroed")
        eps_ok, bias_ok = sem("eps_ok"), sem("bias_ok")
        h_ready, squares, rms_ok, normed = sem("h_ready"), sem("squares"), sem("rms_ok"), sem("normed")
        xt_ps, xh_ok, xl_ok, acc_first = sem("xt_ps"), sem("xh_ok"), sem("xl_ok"), sem("acc_first")
        evac_a, evac_d = sem("evac_a"), sem("evac_d")
        f1_ps, ut_a, ut_d, f2_ps, yb_h, yb_l = sem("f1_ps"), sem("ut_a"), sem("ut_d"), sem("f2_ps"), sem("yb_h"), sem("yb_l")
        conv_ok, lru_ps, lru_tanh, lru_dec, mult_in, mult_ok, scanned = (
            sem("conv_ok"), sem("lru_ps"), sem("lru_tanh"), sem("lru_dec"), sem("mult_in"), sem("mult_ok"), sem("scanned"))
        gelu_in, gelu_t, yc_ok, yc_h, yc_l = sem("gelu_in"), sem("gelu_t"), sem("yc_ok"), sem("yc_h"), sem("yc_l")
        s_ps, s_max, p_exp, p_norm, pt_ps, pt_ok, av_ps, ya_h, ya_l = (
            sem("s_ps"), sem("s_max"), sem("p_exp"), sem("p_norm"), sem("pt_ps"), sem("pt_ok"), sem("av_ps"), sem("ya_h"), sem("ya_l"))
        merged, mh_ok, ml_ok = sem("merged"), sem("mh_ok"), sem("ml_ok")
        silu_ok, prod_ok, ah_ok, al_ok, at_ps = sem("silu_ok"), sem("prod_ok"), sem("ah_ok"), sem("al_ok"), sem("at_ps")
        hnh_ok, hnl_dve, hnl_pool, xt_a, xt_d, lg_ps, lg_row, lg_t, lg_d, w2_ok, mask_ok, comb_ok, pos_ps, cnt_ps, cnt_ok = (
            sem("hnh_ok"), sem("hnl_dve"), sem("hnl_pool"), sem("xt_a"), sem("xt_d"), sem("lg_ps"), sem("lg_row"), sem("lg_t"), sem("lg_d"), sem("w2_ok"), sem("mask_ok"), sem("comb_ok"), sem("pos_ps"),
            sem("cnt_ps"), sem("cnt_ok"))
        g_ok, gr_ps, xr_a, xr_d, gth_ps, xgh_ok, xgl_ok, gt_ps, gt_ok, slot_zero, ysh_ok, ysl_ok, sc_ps, sc_add = (
            sem("g_ok"), sem("gr_ps"), sem("xr_a"), sem("xr_d"), sem("gth_ps"), sem("xgh_ok"), sem("xgl_ok"), sem("gt_ps"), sem("gt_ok"), sem("slot_zero"),
            sem("ysh_ok"), sem("ysl_ok"), sem("sc_ps"), sem("sc_add"))
        out_ok, stored = sem("out_ok"), sem("stored")
        dve_link, act_link, pool_link = sem("dve_link"), sem("act_link"), sem("pool_link")

        ACT_EVACS = [g not in (UF, V) for g in GROUPS] + [False] * len(BRANCHES)
        DVE_EVACS = [g < GATE0 for g in GROUPS] + [True] * len(BRANCHES)

        def group_end(l, n):
            return BASE_MIX[l] + (4 * (n + 1) if n < len(GROUPS) else U_IN + 2 * (n + 1 - len(GROUPS)))

        def evacs(which, l, n):
            return l * sum(which) + sum(which[:n + 1])

        def ff_count(p, e, s):
            return FF_STEPS + E * FE_STEPS * p + FE_STEPS * e + s + 1

        def at_count(p, s):
            return E * FE_STEPS * p + s + 1

        def place(u):
            if u < BASE_MOE:
                return raw[:, u % RAW, :], raw_full[u % RAW], 16 * (u // RAW + 1)
            turn, j = (u - BASE_MOE) // RAW_MOE, (u - BASE_MOE) % RAW_MOE
            if j < RAW:
                return raw[:, (BASE_MOE + j) % RAW, :], raw_full[(BASE_MOE + j) % RAW], 16 * ((BASE_MOE + j) // RAW + turn + 1)
            return mix[:, UNIT * (j - RAW):UNIT * (j - RAW + 1)], mix_full[j - RAW], 16 * (turn + 1)

        block = ctx.enter_context(nc.Block())

        @block.sync
        def _(sp):
            def load(base, k, src, i=0, per=0):
                u = base + k
                ring = RAW_MOE if u >= BASE_MOE else RAW
                dst, arrived, _ = place(u)
                if u >= ring:
                    sp.wait_ge(lo_dve, i * per + (u - ring + 1))
                    sp.wait_ge(lo_pool, i * per + (u - ring + 1))
                sp.dma_start(dst.rearrange("p (k n) -> p k n", k=src.shape[1]), src).then_inc(arrived, 16)

            def square(w, r, c):
                return w[256 * r:256 * r + 256, 512 * c:512 * c + 512].rearrange("(k p) n -> p k n", p=P)

            def wide(w, r):
                return w[P * r:P * r + P, :].rearrange("(k p) n -> p k n", p=P)

            def load_tables(l, k):
                if k < 4:
                    g, hh = k // 2, k % 2
                    w = (lru_wa, lru_wx)[g]
                    for d in range(2):
                        sp.dma_start(wlru[hh * HD:(hh + 1) * HD, d, g, :, :],
                                     w[l, d, hh::2, :, :].rearrange("m c o -> c m o")).then_inc(wlru_in, 16)
                elif k < 4 + HEADS:
                    hd = k - 4
                    for r in range(2):
                        src = bass.AP(rpb.tensor, ((l * HEADS + hd) * (2 * KH_MAX - 1) + KH_MAX - ROWS + 1 - r) * P,
                                      [[1, GRID_W], [P, BT_SLOTS], [1, GRID_W]])
                        sp.dma_start(bias_t[r * GRID_W:(r + 1) * GRID_W, hd * BT_SLOTS:(hd + 1) * BT_SLOTS, :],
                                     src).then_inc(bias_in, 16)

            def load_vectors():
                sp.dma_start(rows_in[0:2 * NB, 0, :], b_in.rearrange("l (j p) -> (l j) p", p=P)).then_inc(vec_in, 16)
                r = 0
                for src, n in ((conv_w.rearrange("l t (m p) -> (l t m) p", p=P), O_CB - O_CW),
                               (conv_b.rearrange("l (m p) -> (l m) p", p=P), 2 * BC),
                               (lru_ba.rearrange("l d (m p) -> (l d m) p", p=P), 4 * BC),
                               (lru_bx.rearrange("l d (m p) -> (l d m) p", p=P), 4 * BC),
                               (lru_lambda.rearrange("l d (m p) -> (l d m) p", p=P), 4 * BC)):
                    sp.dma_start(rows_in[r:r + n, 1, :], src).then_inc(vec_in, 16)
                    r += n
                sp.dma_start(cst[:, P:], consts[:, P:]).then_inc(const_in, 16)
                sp.dma_start(rw[:, :, :], router_w[0].rearrange("(c p) e -> p c e", p=P)).then_inc(rw_in, 16)

            def mixer(l):
                if l:
                    sp.wait_ge(s_max, NA * l)
                    sp.wait_ge(lru_ps, 2 * l)
                k = 0
                for g in GROUPS:
                    for r in range(4):
                        load(BASE_MIX[l], k, square(w_in[l], r, g))
                        load_tables(l, k)
                        k += 1
                        if l == 0 and k == 3:
                            load_vectors()
                for dg, b in BRANCHES:
                    for r in range(2):
                        load(BASE_MIX[l], k, square(w_branch[l, b], r, dg))
                        k += 1
                for r in range(U_OUT):
                    load(BASE_MIX[l], k, wide(w_out[l], r))
                    k += 1

            def dense():
                gu, down = ffn_w_gu[0], ffn_w_down[0]
                for r in range(4):
                    load(BASE_FF, r, square(gu, r, 0))
                for r in range(4):
                    load(BASE_FF, 4 + r, square(gu, r, FF_STEPS))
                with sp.Fori(0, FF_STEPS - 1) as i:
                    for half in range(2):
                        for r in range(4):
                            c = (i + (1 + half * FF_STEPS)) * 512
                            src = gu[256 * r:256 * r + 256, bass.ds(c, 512)].rearrange("(k p) n -> p k n", p=P)
                            load(BASE_FF + 8, 4 * half + r, src, i, 12)
                    for r in range(4):
                        src = down[bass.ds(i * 512 + r * P, P), :].rearrange("(k p) n -> p k n", p=P)
                        load(BASE_FF + 8, 8 + r, src, i, 12)
                for r in range(4):
                    load(BASE_FF, U_FF - 4 + r, wide(down, 4 * (FF_STEPS - 1) + r))

            def experts(p):
                base = BASE_MOE + p * E * U_EX
                if p == 0:
                    sp.wait_ge(lo_dve, BASE_MOE)
                    sp.wait_ge(lo_pool, BASE_MOE)
                with sp.Fori(0, E) as e:
                    k = 0
                    gu, dn = moe_w_gu[0, e], moe_w_down[0, e]
                    for what, s in (("gu", 0), ("gu", 1), ("dn", 0), ("gu", 2), ("dn", 1), ("dn", 2)):
                        if what == "gu":
                            for c in (s, FE_STEPS + s):
                                for r in range(4):
                                    load(base, k, square(gu, r, c), e, U_EX)
                                    k += 1
                        else:
                            for r in range(4):
                                load(base, k, wide(dn, 4 * s + r), e, U_EX)
                                k += 1

            sp.dma_start(h[:, 0, :], x[0, 0:P, :]).then_inc(x_in[0], 16)
            sp.dma_start(cst[:, 0:P], consts[:, 0:P]).then_inc(ident_in, 16)
            sp.dma_start(h[:, 1, :], x[0, P:2 * P, :]).then_inc(x_in[1], 16)
            mixer(0)
            dense()
            mixer(1)
            experts(0)
            sp.wait_ge(cnt_ok, 1)
            most = sp.value_load(cnt_i[0:1, 0:1], min_val=0, max_val=SEQ)
            with sp.If(most > FIRST_SLOTS):
                experts(1)
            for t in range(TT):
                sp.wait_ge(out_ok, t + 1)
                sp.dma_start(out[0, t * P:(t + 1) * P, :], hn[:, t, :]).then_inc(stored, 16)
            sp.wait_ge(stored, 16 * TT)

        @block.gpsimd
        def _(pool):
            def lo(base, k, i=0, per=0):
                u = base + k
                cut = CUT_MOE if base >= BASE_MOE else CUT
                pool.wait_ge(hi_done, i * per + (u + 1))
                pool.tensor_tensor(w_lo[:, u % RH, cut:], place(u)[0][:, cut:],
                                   w_hi[:, u % RH, cut:].bitcast(F32), ALU.subtract).then_inc(lo_pool, 1)

            def load_row(src, offset, read=None, count=0):
                if read is not None:
                    pool.wait_ge(read, count)
                pool.dma_start(row[:, :], bass.AP(src.tensor, offset, [[0, P], [1, D]])).then_inc(row_in, 16)

            def mask_tables(l, hp):
                pool.wait_ge(const_in, 16)
                pool.wait_ge(bias_in, 16 * 2 * (HEADS * l + 2 * hp + 2))
                n = 2 * BT_SLOTS
                m = cst[:, C_MASK:C_MASK + GRID_W].unsqueeze(1).to_broadcast([P, n, GRID_W])
                pool.tensor_tensor(bias_t[:, n * hp:n * hp + n, :], bias_t[:, n * hp:n * hp + n, :], m,
                                   ALU.add).then_inc(bias_ok, 1)

            def mixer(l):
                for k in range(U_MIX):
                    if k == 3:
                        load_row(b_in, l * IN_COLS + 2 * BR, normed, 2 * TT * (2 * l + 1))
                    if k in AT_MASK:
                        mask_tables(l, AT_MASK.index(k))
                    if k == 28:
                        load_row(norm_ffn_g, l * D, evac_d, evacs(DVE_EVACS, l, GROUPS.index(V)))
                    lo(BASE_MIX[l], k)

            def dense():
                for k in range(8):
                    lo(BASE_FF, k)
                load_row(norm_mix_g, D, normed, 2 * TT * 2)
                with pool.Fori(0, FF_STEPS - 1) as i:
                    for k in range(12):
                        lo(BASE_FF + 8, k, i, 12)
                for k in range(4):
                    lo(BASE_FF + U_FF - 4, k)

            def experts(p):
                with pool.Fori(0, E) as e:
                    for k in range(U_EX):
                        lo(BASE_MOE + p * E * U_EX, k, e, U_EX)

            load_row(norm_mix_g, 0)
            pool.memset(ux_t[:, :, :], 0.0).then_inc(zeroed, 1)
            mixer(0)
            dense()
            mixer(1)
            load_row(final_g, 0, normed, 2 * TT * 4)
            pool.wait_ge(hnh_ok, 1)
            pool.tensor_tensor(ylf[:, 0:D], gflat[:, 0:D], yhf[:, 0:D].bitcast(F32),
                               ALU.subtract).then_inc(hnl_pool, 1)
            experts(0)
            pool.wait_ge(cnt_ok, 1)
            most = pool.value_load(cnt_i[0:1, 0:1], min_val=0, max_val=SEQ)
            with pool.If(most > FIRST_SLOTS):
                experts(1)

        @block.scalar
        def _(act):
            links = [0]

            def link(ins):
                links[0] += 1
                ins.then_inc(act_link, 1)
                act.wait_ge(act_link, links[0])

            def hi(base, k, i=0, per=0):
                u = base + k
                ring = RAW_MOE if u >= BASE_MOE else RAW
                src, arrived, count = place(u)
                act.wait_ge(arrived, 16 * (per // ring) * i + count)
                if u >= RH:
                    act.wait_ge(unit_used, i * per + (u - RH + 1))
                act.activation(w_hi[:, u % RH, :], src, ACT.Copy).then_inc(hi_done, 1)

            def norm(n):
                if n == 0:
                    act.wait_ge(eps_ok, 1)
                link(act.activation(table_in, eps_t[:, 0:1], ACT.Sqrt))
                for t in range(TT):
                    if n == 0:
                        act.wait_ge(x_in[t], 16)
                    else:
                        act.wait_ge(h_ready, TT * (n - 1) + t + 1)
                    act.activation(junk[:, t, :], h[:, t, :], ACT.Square, accum_out=ss[:, t:t + 1]).then_inc(squares, 1)
                    act.wait_ge(squares, TT * n + t + 1)
                    act.activation(rms[:, t:t + 1], ss[:, t:t + 1], ACT.Sqrt, scale=1.0 / D,
                                   bias=eps_t[:, 0:1]).then_inc(rms_ok, 1)

            def norm_hi(n):
                for b in range(4):
                    act.wait_ge(xt_ps, 4 * n + b + 1)
                    act.activation(xhf[:, 512 * b:512 * b + 512], ps[:, 4 + b, :], ACT.Copy).then_inc(xh_ok, 1)

            def mixer(l):
                B = BASE_MIX[l]
                if l == 0:
                    norm(0)
                for k in range(AHEAD):
                    hi(B, k)
                if l:
                    norm(2 * l)
                norm_hi(2 * l)
                for k in range(U_MIX):
                    if k + AHEAD < U_MIX:
                        hi(B, k + AHEAD)
                    if l == 0 and k == 1:
                        act.wait_ge(col_ok, 1)
                        link(act.activation(lam_w[:, 0, :], col[:, O_LAM:O_LAM + 16], ACT.Abs))
                        act.activation(lam_w[:, 1, :], lam_w[:, 0, :], ACT.Exp, scale=-1.0).then_inc(lam_act, 1)
                    if l == 0 and k == 8:
                        act.wait_ge(col2_ok, 1)
                        act.wait_ge(zeroed, 1)
                    n = k // 4 - 1
                    if k <= U_IN and k % 4 == 0 and n >= 0 and ACT_EVACS[n]:
                        g = GROUPS[n]
                        act.wait_ge(unit_used, group_end(l, n))
                        b0 = 2 * (n % 2)
                        bc = l * NB + 4 * g
                        if g == Q:
                            for m in range(2):
                                i = act.activation(q_t[:, m, :], ps[:, b0, SEQ * m:SEQ * m + SEQ], ACT.Identity,
                                                   scale=SCALE, bias=col2[:, O_BQ + 4 * l + m:O_BQ + 4 * l + m + 1])
                        elif g in (K, UX, UG):
                            for m in range(2):
                                dst = {K: k_t[:, m, :], UX: ux_t[:, m, 2:2 + SEQ],
                                       UG: ug_t[:, SEQ * m:SEQ * m + SEQ]}[g]
                                i = act.activation(dst, ps[:, b0, SEQ * m:SEQ * m + SEQ], ACT.Identity,
                                                   bias=col[:, bc + m:bc + m + 1])
                        else:
                            for m in range(4):
                                gb = col2[:, O_GB + 24 * l + 4 * (g - GATE0) + m:O_GB + 24 * l + 4 * (g - GATE0) + m + 1]
                                i = act.activation(gates[:, 4 * (g - GATE0) + m, :],
                                                   ps[:, b0 + m // 2, SEQ * (m % 2):SEQ * (m % 2) + SEQ],
                                                   ACT.Tanh, scale=0.5, bias=gb)
                        i.then_inc(evac_a, 1)
                    if k == AT_F1:
                        act.wait_ge(f1_ps, l + 1)
                        for m in range(2):
                            i = act.activation(lru[:, 0, 512 * m:512 * m + 512], ps[:, 4 + m, :], ACT.Copy)
                        i.then_inc(ut_a, 1)
                    if k == AT_F2:
                        act.wait_ge(f2_ps, l + 1)
                        for b in range(2):
                            act.activation(yhf[:, D + 512 * b:D + 512 * b + 512], ps[:, 4 + b, :],
                                           ACT.Copy).then_inc(yb_h, 1)
                    for d, at in ((0, AT_LF), (1, AT_LB)):
                        if k == at or k == at + 1:
                            g = k - at
                            act.wait_ge(lru_ps, 2 * l + d + 1)
                            if d:
                                act.wait_ge(scanned, 2 * l + 1)
                            for m in range(BC):
                                o = (O_HBA, O_HBX)[g] + (2 * l + d) * BC + m
                                i = act.activation(lru[:, g, SEQ * m:SEQ * m + SEQ],
                                                   ps[:, 4 + 2 * g + m // 2, SEQ * (m % 2):SEQ * (m % 2) + SEQ],
                                                   ACT.Tanh, scale=0.5, bias=col2[:, o:o + 1])
                            i.then_inc(lru_tanh, 1)
                        if k == at + 1:
                            act.wait_ge(lru_tanh, 2 * (2 * l + d) + 1)
                            dst = uf_t[:, :] if d else lru[:, 2, :]
                            for m in range(BC):
                                o = (2 * l + d) * BC + m
                                i = act.activation(dst[:, SEQ * m:SEQ * m + SEQ], lru[:, 0, SEQ * m:SEQ * m + SEQ],
                                                   ACT.Tanh, scale=col2[:, O_SP + o:O_SP + o + 1],
                                                   bias=col2[:, O_SP + o:O_SP + o + 1])
                            i.then_inc(lru_dec, 1)
                        if k == at + 2:
                            act.wait_ge(lru_dec, 2 * (2 * l + d) + 1)
                            for m in range(BC):
                                o = (2 * l + d) * BC + m
                                i = act.activation(lru[:, 0, SEQ * m:SEQ * m + SEQ], lru[:, 0, SEQ * m:SEQ * m + SEQ],
                                                   ACT.Exp, scale=col2[:, O_NSP + o:O_NSP + o + 1],
                                                   bias=col2[:, O_NSP + o:O_NSP + o + 1])
                            i.then_inc(lru_dec, 1)
                        if k == at + 4:
                            dst = uf_t[:, :] if d else lru[:, 2, :]
                            act.wait_ge(mult_in, 2 * l + d + 1)
                            act.activation(dst, dst, ACT.Sqrt).then_inc(mult_ok, 1)
                    if k == AT_LB + 9:
                        act.wait_ge(gelu_in, l + 1)
                        act.activation(lru[:, 0, :], lru[:, 0, :], ACT.Tanh, scale=GELU_C).then_inc(gelu_t, 1)
                    if k == AT_LB + 12:
                        act.wait_ge(yc_ok, l + 1)
                        act.activation(yhf[:, 2 * D:3 * D], lru[:, 1, :], ACT.Copy, scale=0.5).then_inc(yc_h, 1)
                    j = k - AT_ATT
                    if 2 <= j < NA + 2:
                        act.wait_ge(pt_ps, NA * l + j - 1)
                        if j - 2 >= 2:
                            act.wait_ge(av_ps, NA * l + j - 3)
                        act.activation(pt_t[:, j % 2, :], ps[:, 5, 0:SEQ], ACT.Copy).then_inc(pt_ok, 1)
                    if 0 <= j < NA:
                        act.wait_ge(s_max, NA * l + j + 1)
                        act.activation(p_t[:, j % 2, :], p_t[:, j % 2, :], ACT.Exp, bias=nmax[:, j % 2:j % 2 + 1],
                                       accum_out=rsum[:, j % 2:j % 2 + 1]).then_inc(p_exp, 1)
                    if j >= 3 and (j - 3) % 4 == 3 and j - 3 < NA:
                        hp = (j - 3) // 4
                        act.wait_ge(av_ps, NA * l + j - 2)
                        act.activation(yh[:, hp, :], ps[:, 6 + hp % 2, 0:SEQ], ACT.Copy).then_inc(ya_h, 1)
                    for dg in range(2):
                        if k == U_IN + 6 * (dg + 1) + 1:
                            for b in range(2):
                                act.wait_ge(merged, 4 * l + 2 * dg + b + 1)
                                at = 1024 * dg + 512 * b
                                act.activation(xhf[:, at:at + 512], gflat[:, at:at + 512],
                                               ACT.Copy, scale=0.5).then_inc(mh_ok, 1)

            def step_hi(n, dst, i=0, per=0):
                act.wait_ge(prod_ok, i * per + n)
                act.activation(dst, prod_t[:, 0:dst.shape[1]], ACT.Copy).then_inc(ah_ok, 1)

            def dense():
                B = BASE_FF
                for k in range(AHEAD):
                    hi(B, k)
                norm(1)
                norm_hi(1)

                def silu(n, g_end, i=0):
                    act.wait_ge(unit_used, i * 12 + g_end)
                    if n > 1:
                        act.wait_ge(prod_ok, i + (n - 1))
                    for b in range(2):
                        ins = act.activation(silu_t[:, 512 * b:512 * b + 512], ps[:, b, :], ACT.Silu)
                    ins.then_inc(silu_ok, 1)

                for k in range(AHEAD, 8):
                    hi(B, k)
                silu(1, B + 4)
                with act.Fori(0, FF_STEPS - 1) as i:
                    for k in range(12):
                        hi(B + 8, k, i, 12)
                        if k == 2:
                            act.wait_ge(unit_used, i * 12 + (B + 8))
                            step_hi(1, yhf[:, 0:1024], i, 1)
                        if k == 7:
                            silu(2, B + 12, i)
                for k in range(4):
                    hi(B + U_FF - 4, k)
                    if k == 1:
                        act.wait_ge(unit_used, B + U_FF - 4)
                        step_hi(FF_STEPS, yhf[:, 0:1024])

            def experts(p):
                B = BASE_MOE + p * E * U_EX
                ff = E * FE_STEPS

                def silu(e, s):
                    act.wait_ge(unit_used, e * U_EX + (B + (4, 12, 24)[s]))
                    act.wait_ge(prod_ok, e * FE_STEPS + (ff_count(p, 0, s) - 1))
                    act.activation(silu_t[:, 0:512], ps[:, 2 * (s % 2), :], ACT.Silu).then_inc(silu_ok, 1)

                def gather_rows(n, e):
                    act.wait_ge(gr_ps, e * 2 + (2 * n + 1))
                    act.activation(xrow[:, 0:512], ps[:, 6, :], ACT.Copy).then_inc(xr_a, 1)

                def gather_hi(n, e):
                    for b in range(2):
                        act.wait_ge(gth_ps, e * 2 + (2 * n + b + 1))
                        act.activation(xg_h[:, 512 * b:512 * b + 512], ps[:, 6 + b, :], ACT.Copy).then_inc(xgh_ok, 1)

                def rows_hi(n, e):
                    act.wait_ge(unit_used, e * U_EX + (B + (E * U_EX if n % (E + 1) == 0 else 0)))
                    for b in range(2):
                        ins = act.activation(ys_h[:, 512 * b:512 * b + 512], ps[:, 4 + b, :], ACT.Copy,
                                             scale=slot_w)
                        ins.then_inc(ysh_ok, 1)

                def product_hi(e, s):
                    act.wait_ge(at_ps, e * FE_STEPS + at_count(p, s))
                    o = 2048 + 512 * (s % 2)
                    act.activation(yhf[:, o:o + 512], ps[:, 2 * (s % 2), :], ACT.Copy).then_inc(ah_ok, 1)

                if p == 0:
                    for t in range(TT):
                        act.wait_ge(normed, 2 * (TT * 3 + t + 1))
                        act.activation(yhf[:, D * t:D * t + D], gflat[:, D * t:D * t + D], ACT.Copy).then_inc(hnh_ok, 1)
                        if t == 0:
                            for b in range(2):
                                act.wait_ge(xt_ps, 4 * 3 + b + 1)
                                act.activation(xt_full[:, 512 * b:512 * b + 512], ps[:, 4 + b, :],
                                               ACT.Copy).then_inc(xt_a, 1)
                    act.activation(table_in, eps_t[:, 0:1], ACT.Exp)
                    act.wait_ge(lg_d, 1)
                    act.activation(wtop[:, :, 2:3], wtop[:, :, 1:2], ACT.Exp).then_inc(w2_ok, 1)
                gather_rows((E + 1) * p, 0)
                gather_hi((E + 1) * p, 0)
                act.wait_ge(slot_zero, p + 1)
                with act.Fori(0, E) as e:
                    for k in range(AHEAD):
                        hi(B, k, e, U_EX)
                    rows_hi((E + 1) * p + 1, e)
                    for k in range(AHEAD, U_EX):
                        hi(B, k, e, U_EX)
                        if k == 4 + AHEAD:
                            silu(e, 0)
                        if k == 11 + AHEAD:
                            product_hi(e, 0)
                        if k == 12 + AHEAD:
                            silu(e, 1)
                        if k == 16 + AHEAD:
                            act.wait_ge(gt_ps, e + (E * p + 1))
                            act.activation(gt_t[:, :, :].rearrange("p t s -> p (t s)"), ps[:, 6, 0:2 * P], ACT.Copy)\
                               .then_inc(gt_ok, 1)
                            act.activation(slot_w, ps[:, 6, 2 * P:2 * P + 1], ACT.Copy).then_inc(gt_ok, 1)
                        if k == 20 + AHEAD:
                            product_hi(e, 1)
                        if k == 24 + AHEAD:
                            silu(e, 2)
                        if k == 25 + AHEAD:
                            gather_rows((E + 1) * p + 1, e)
                        if k == 28 + AHEAD:
                            gather_hi((E + 1) * p + 1, e)
                        if k == 29 + AHEAD:
                            product_hi(e, 2)
                rows_hi((E + 1) * (p + 1), 0)

            mixer(0)
            dense()
            mixer(1)
            norm(3)
            experts(0)
            act.wait_ge(cnt_ok, 1)
            most = act.value_load(cnt_i[0:1, 0:1], min_val=0, max_val=SEQ)
            with act.If(most > FIRST_SLOTS):
                experts(1)
            norm(4)

        @block.vector
        def _(dve):
            links = [0]

            def link(ins):
                links[0] += 1
                ins.then_inc(dve_link, 1)
                dve.wait_ge(dve_link, links[0])

            def lo(base, k, i=0, per=0):
                u = base + k
                cut = CUT_MOE if base >= BASE_MOE else CUT
                dve.wait_ge(hi_done, i * per + (u + 1))
                dve.tensor_tensor(w_lo[:, u % RH, 0:cut], place(u)[0][:, 0:cut],
                                  w_hi[:, u % RH, 0:cut].bitcast(F32), ALU.subtract).then_inc(lo_dve, 1)

            def norm(n):
                for t in range(TT):
                    dve.wait_ge(rms_ok, TT * n + t + 1)
                    link(dve.reciprocal(rinv[:, t:t + 1], rms[:, t:t + 1]))
                    if t == 0:
                        dve.wait_ge(row_in, 16 * ({0: 0, 1: 2, 2: 3, 3: 5, 4: 6}[n] + 1))
                    for half in range(2):
                        q = slice(512 * half, 512 * half + 512)
                        ins = dve.scalar_tensor_tensor(out=hn[:, t, q], in0=h[:, t, q], scalar=rinv[:, t:t + 1],
                                                       in1=row[:, q], op0=ALU.mult, op1=ALU.mult)
                        if n < 4:
                            ins.then_inc(normed, 1)
                    if n == 4:
                        ins.then_inc(out_ok, 1)

            def norm_lo(n):
                for b in range(4):
                    dve.wait_ge(xh_ok, 4 * n + b + 1)
                    dve.tensor_tensor(xlf[:, 512 * b:512 * b + 512], ps[:, 4 + b, :],
                                      xhf[:, 512 * b:512 * b + 512].bitcast(F32), ALU.subtract).then_inc(xl_ok, 1)

            def add_acc(n, end):
                for t in range(TT):
                    if t == 0:
                        dve.wait_ge(acc_first, n)
                    else:
                        dve.wait_ge(unit_used, end)
                    for half in range(2):
                        ins = dve.tensor_tensor(h[:, t, 512 * half:512 * half + 512], ps[:, 4 + 2 * t + half, :],
                                                h[:, t, 512 * half:512 * half + 512], ALU.add)
                    ins.then_inc(h_ready, 1)

            def set_up_columns():
                dve.wait_ge(const_in, 16)
                dve.wait_ge(vec_t, 1)
                dve.tensor_copy(col[:, 0:2 * NB], ps[:, 2, 0:2 * NB])
                link(dve.tensor_copy(col[:, 2 * NB:N_COL], ps[:, 3, 0:N_COL - 2 * NB]))
                dve.tensor_scalar(col2[:, O_HBA:O_HBA + 32], col[:, O_BA:O_BA + 32], 0.5, None, ALU.mult)
                for l in range(2):
                    dve.tensor_scalar(col2[:, O_BQ + 4 * l:O_BQ + 4 * l + 4], col[:, l * NB + 4 * Q:l * NB + 4 * Q + 4],
                                      SCALE, None, ALU.mult)
                    dve.tensor_scalar(col2[:, O_GB + 24 * l:O_GB + 24 * l + 24],
                                      col[:, l * NB + 4 * GATE0:l * NB + 4 * GATE0 + 24], 0.5, None, ALU.mult)
                dve.tensor_scalar(lam_w[:, 5, :], col[:, O_LAM:O_LAM + 16], -1.0, 0.0, ALU.mult, ALU.max).then_inc(col_ok, 1)

            def set_up_decay():
                dve.wait_ge(lam_act, 1)
                link(dve.tensor_scalar(lam_w[:, 2, :], lam_w[:, 1, :], 2.0, None, ALU.add))
                link(dve.reciprocal(lam_w[:, 2, :], lam_w[:, 2, :]))
                link(dve.tensor_tensor(lam_w[:, 2, :], lam_w[:, 2, :], lam_w[:, 1, :], ALU.mult))
                link(dve.tensor_tensor(lam_w[:, 3, :], lam_w[:, 2, :], lam_w[:, 2, :], ALU.mult))
                link(dve.tensor_scalar(lam_w[:, 4, :], lam_w[:, 3, :], 1.0 / 19, None, ALU.mult))
                for odd in range(17, 1, -2):
                    link(dve.scalar_tensor_tensor(out=lam_w[:, 4, :], in0=lam_w[:, 4, :], scalar=1.0 / odd,
                                                  in1=lam_w[:, 3, :], op0=ALU.add, op1=ALU.mult))
                link(dve.scalar_tensor_tensor(out=lam_w[:, 4, :], in0=lam_w[:, 4, :], scalar=1.0, in1=lam_w[:, 2, :],
                                              op0=ALU.add, op1=ALU.mult))
                link(dve.scalar_tensor_tensor(out=lam_w[:, 4, :], in0=lam_w[:, 4, :], scalar=2.0, in1=lam_w[:, 5, :],
                                              op0=ALU.mult, op1=ALU.add))
                dve.tensor_scalar(col2[:, O_SP:O_SP + 16], lam_w[:, 4, :], 4.0, None, ALU.mult)
                dve.tensor_scalar(col2[:, O_NSP:O_NSP + 16], lam_w[:, 4, :], -4.0, None, ALU.mult).then_inc(col2_ok, 1)

            def mixer(l):
                B = BASE_MIX[l]
                if l == 0:
                    for k in range(AHEAD):
                        lo(B, k)
                norm(2 * l)
                norm_lo(2 * l)
                for k in range(U_MIX):
                    if k + AHEAD < U_MIX:
                        lo(B, k + AHEAD)
                    if l == 0 and k == 1:
                        set_up_columns()
                    if l == 0 and k == 2:
                        set_up_decay()
                    n = k // 4 - 1
                    if k <= U_IN and k % 4 == 0 and n >= 0 and DVE_EVACS[n]:
                        g = GROUPS[n]
                        dve.wait_ge(unit_used, group_end(l, n))
                        b0 = 2 * (n % 2)
                        bc = l * NB + 4 * g
                        if g in (UF, V):
                            dve.wait_ge(row_in, 16 * (3 * l + 2))
                            for t in range(TT):
                                dst = uf_t[:, BR * t:BR * t + BR] if g == UF else v_t[:, t, :]
                                off = BR if g == UF else 0
                                i = dve.tensor_tensor(dst, ps[:, b0 + t, :], row[:, off:off + BR], ALU.add)
                            i.then_inc(evac_d, 1)
                        else:
                            for m in range(2, 4):
                                src = ps[:, b0 + 1, SEQ * (m - 2):SEQ * (m - 2) + SEQ]
                                if g == Q:
                                    i = dve.tensor_scalar(q_t[:, m, :], src, col[:, bc + m:bc + m + 1], SCALE,
                                                          ALU.add, ALU.mult)
                                else:
                                    dst = {K: k_t[:, m, :], UX: ux_t[:, m, 2:2 + SEQ],
                                           UG: ug_t[:, SEQ * m:SEQ * m + SEQ]}[g]
                                    if g == UX and l == 0:
                                        dve.wait_ge(zeroed, 1)
                                    i = dve.tensor_scalar(dst, src, col[:, bc + m:bc + m + 1], None, ALU.add)
                            i.then_inc(evac_d, 1)
                    if AT_CONV <= k < AT_CONV + 4:
                        tap = k - AT_CONV
                        if tap == 0:
                            dve.wait_ge(evac_a, evacs(ACT_EVACS, l, 1))
                            dve.wait_ge(evac_d, evacs(DVE_EVACS, l, 1))
                            if l:
                                dve.wait_ge(lru_ps, 2 * l)
                        for m in range(BC):
                            w = col[:, O_CW + (4 * l + tap) * BC + m:O_CW + (4 * l + tap) * BC + m + 1]
                            src = ux_t[:, m, tap:tap + SEQ]
                            if tap == 0:
                                o = O_CB + l * BC + m
                                i = dve.tensor_scalar(conv_t[:, m, :], src, w, col[:, o:o + 1], ALU.mult, ALU.add)
                            else:
                                i = dve.scalar_tensor_tensor(out=conv_t[:, m, :], in0=src, scalar=w,
                                                             in1=conv_t[:, m, :], op0=ALU.mult, op1=ALU.add)
                        if tap < 3:
                            link(i)
                        else:
                            i.then_inc(conv_ok, 1)
                    if k == AT_F1:
                        dve.wait_ge(f1_ps, l + 1)
                        for m in range(2):
                            i = dve.tensor_copy(lru[:, 1, 512 * m:512 * m + 512], ps[:, 6 + m, :])
                        i.then_inc(ut_d, 1)
                    if k == AT_F2:
                        for b in range(2):
                            dve.wait_ge(yb_h, 2 * l + b + 1)
                            at = D + 512 * b
                            i = dve.tensor_tensor(ylf[:, at:at + 512], ps[:, 4 + b, :],
                                                  yhf[:, at:at + 512].bitcast(F32), ALU.subtract)
                        i.then_inc(yb_l, 1)
                    j = k - AT_ATT
                    if 0 <= j < NA:
                        hp, t, hh = UNITS_ATT[j]
                        dve.wait_ge(s_ps, NA * l + j + 1)
                        dve.wait_ge(bias_ok, 4 * l + hp + 1)
                        if j >= 2:
                            dve.wait_ge(pt_ps, NA * l + j - 1)
                        s0 = (2 * hp + hh) * BT_SLOTS + 2 - 2 * t
                        bias = bias_t[:, s0:s0 + ROWS, ::-1]
                        b2 = j % 2
                        link(dve.tensor_tensor(p_t[:, b2, :].rearrange("p (r c) -> p r c", r=ROWS),
                                               ps[:, 4, 0:SEQ].rearrange("p (r c) -> p r c", r=ROWS), bias, ALU.add))
                        link(dve.tensor_reduce(smax[:, b2:b2 + 1], p_t[:, b2, :], AX_X, ALU.max))
                        dve.tensor_scalar(nmax[:, b2:b2 + 1], smax[:, b2:b2 + 1], -1.0, None,
                                          ALU.mult).then_inc(s_max, 1)
                    if 1 <= j < NA + 1:
                        b2 = (j - 1) % 2
                        dve.wait_ge(p_exp, NA * l + j)
                        link(dve.reciprocal(rrec[:, b2:b2 + 1], rsum[:, b2:b2 + 1]))
                        dve.tensor_scalar(p_t[:, b2, :], p_t[:, b2, :], rrec[:, b2:b2 + 1], None,
                                          ALU.mult).then_inc(p_norm, 1)
                    if j >= 3 and (j - 3) % 4 == 3 and j - 3 < NA:
                        hp = (j - 3) // 4
                        dve.wait_ge(ya_h, 4 * l + hp + 1)
                        dve.tensor_tensor(yl[:, hp, :], ps[:, 6 + hp % 2, 0:SEQ], yh[:, hp, :].bitcast(F32),
                                          ALU.subtract).then_inc(ya_l, 1)
                    for d, at in ((0, AT_LF), (1, AT_LB)):
                        t_buf = uf_t[:, :] if d else lru[:, 2, :]
                        if k == at + 3:
                            t_3d = t_buf.rearrange("p (m s) -> p m s", m=BC)
                            a_3d = lru[:, 0, :].rearrange("p (m s) -> p m s", m=BC)
                            dve.wait_ge(lru_dec, 2 * (2 * l + d) + 2)
                            link(dve.tensor_tensor(ux_in, a_3d, a_3d, ALU.mult))
                            dve.scalar_tensor_tensor(out=t_3d, in0=ux_in, scalar=1.0, in1=t_3d,
                                                     op0=ALU.add, op1=ALU.mult).then_inc(mult_in, 1)
                        if k == at + 4:
                            dve.wait_ge(lru_tanh, 2 * (2 * l + d + 1))
                            link(dve.scalar_tensor_tensor(out=lru[:, 1, :], in0=lru[:, 1, :], scalar=1.0, in1=cflat,
                                                          op0=ALU.add, op1=ALU.mult))
                        if k == at + 5:
                            first = SEQ - 1 if d else 0
                            dve.wait_ge(mult_ok, 2 * l + d + 1)
                            dve.wait_ge(lru_dec, 2 * (2 * l + d) + 2)
                            dve.memset(t_buf.rearrange("p (m s) -> p m s", m=BC)[:, :, first:first + 1], 1.0)
                            link(dve.memset(lru[:, 0, :].rearrange("p (m s) -> p m s", m=BC)[:, :, first:first + 1], 0.0))
                            link(dve.scalar_tensor_tensor(out=lru[:, 1, :], in0=t_buf, scalar=0.5, in1=lru[:, 1, :],
                                                          op0=ALU.mult, op1=ALU.mult))
                        if k == at + 6:
                            if d:
                                dve.tensor_tensor_scan(t_buf[:, ::-1], lru[:, 0, ::-1], lru[:, 1, ::-1], 0.0,
                                                       ALU.mult, ALU.add).then_inc(scanned, 1)
                            else:
                                dve.tensor_tensor_scan(t_buf, lru[:, 0, :], lru[:, 1, :], 0.0,
                                                       ALU.mult, ALU.add).then_inc(scanned, 1)
                    if k == AT_LB + 7:
                        dve.wait_ge(scanned, 2 * l + 2)
                        dve.wait_ge(evac_a, evacs(ACT_EVACS, l, 5))
                        dve.wait_ge(evac_d, evacs(DVE_EVACS, l, 5))
                        link(dve.tensor_tensor(lru[:, 0, :], ug_t[:, :], ug_t[:, :], ALU.mult))
                        link(dve.tensor_scalar(lru[:, 0, :], lru[:, 0, :], 0.044715, 1.0, ALU.mult, ALU.add))
                    if k == AT_LB + 8:
                        dve.tensor_tensor(lru[:, 0, :], lru[:, 0, :], ug_t[:, :], ALU.mult).then_inc(gelu_in, 1)
                    if k == AT_LB + 9:
                        link(dve.tensor_tensor(lru[:, 2, :], lru[:, 2, :], uf_t[:, :], ALU.add))
                    if k == AT_LB + 10:
                        link(dve.tensor_tensor(lru[:, 2, :], lru[:, 2, :], ug_t[:, :], ALU.mult))
                    if k == AT_LB + 11:
                        dve.wait_ge(gelu_t, l + 1)
                        dve.scalar_tensor_tensor(out=lru[:, 1, :], in0=lru[:, 0, :], scalar=1.0, in1=lru[:, 2, :],
                                                 op0=ALU.add, op1=ALU.mult).then_inc(yc_ok, 1)
                    if k == AT_LB + 13:
                        dve.wait_ge(yc_h, l + 1)
                        dve.scalar_tensor_tensor(out=ylf[:, 2 * D:3 * D], in0=lru[:, 1, :], scalar=0.5,
                                                 in1=yhf[:, 2 * D:3 * D].bitcast(F32), op0=ALU.mult,
                                                 op1=ALU.subtract).then_inc(yc_l, 1)
                    nb = (k - U_IN) // 2 - 1
                    if U_IN < k <= U_IN + U_BR and (k - U_IN) % 2 == 0:
                        dg, br = BRANCHES[nb]
                        n = len(GROUPS) + nb
                        dve.wait_ge(unit_used, group_end(l, n))
                        dve.wait_ge(evac_a, evacs(ACT_EVACS, l, n))
                        for b in range(2):
                            at = br * 2048 + 1024 * dg + 512 * b
                            i = dve.scalar_tensor_tensor(out=gflat[:, at:at + 512], in0=gflat[:, at:at + 512],
                                                         scalar=1.0, in1=ps[:, 2 * (n % 2) + b, :],
                                                         op0=ALU.add, op1=ALU.mult)
                        i.then_inc(evac_d, 1)
                        if nb % 3 == 2:
                            dve.wait_ge(evac_d, evacs(DVE_EVACS, l, n))
                            for b in range(2):
                                at = 1024 * dg + 512 * b
                                i = dve.tensor_tensor(gflat[:, 2048 + at:2048 + at + 512], gflat[:, 2048 + at:2048 + at + 512],
                                                      gflat[:, 4096 + at:4096 + at + 512], ALU.add)
                            link(i)
                            for b in range(2):
                                at = 1024 * dg + 512 * b
                                dve.tensor_tensor(gflat[:, at:at + 512], gflat[:, at:at + 512],
                                                  gflat[:, 2048 + at:2048 + at + 512], ALU.add).then_inc(merged, 1)
                    for dg in range(2):
                        if k == U_IN + 6 * (dg + 1) + 1:
                            for b in range(2):
                                dve.wait_ge(mh_ok, 4 * l + 2 * dg + b + 1)
                                at = 1024 * dg + 512 * b
                                dve.scalar_tensor_tensor(out=xlf[:, at:at + 512], in0=gflat[:, at:at + 512], scalar=0.5,
                                                         in1=xhf[:, at:at + 512].bitcast(F32), op0=ALU.mult,
                                                         op1=ALU.subtract).then_inc(ml_ok, 1)
                if l == 0:
                    for k in range(AHEAD):
                        lo(BASE_FF, k)
                add_acc(2 * l + 1, B + U_MIX)

            def product(n, width, b_u, u_end, i=0, per=0, units=0):
                dve.wait_ge(unit_used, i * units + u_end)
                dve.wait_ge(silu_ok, i * per + n)
                if n > 1:
                    dve.wait_ge(al_ok, i * per + (n - 1))
                for b in range(width // 512):
                    ins = dve.tensor_tensor(prod_t[:, 512 * b:512 * b + 512], ps[:, b_u + b, :],
                                            silu_t[:, 512 * b:512 * b + 512], ALU.mult)
                ins.then_inc(prod_ok, 1)

            def step_lo(n, at, width, i=0, per=0):
                dve.wait_ge(ah_ok, i * per + n)
                dve.tensor_tensor(ylf[:, at:at + width], prod_t[:, 0:width], yhf[:, at:at + width].bitcast(F32),
                                  ALU.subtract).then_inc(al_ok, 1)

            def dense():
                B = BASE_FF
                norm(1)
                norm_lo(1)
                for k in range(AHEAD, 8):
                    lo(B, k)
                with dve.Fori(0, FF_STEPS - 1) as i:
                    for k in range(12):
                        lo(B + 8, k, i, 12)
                        if k == 0:
                            product(1, 1024, 2, B + 8, i, 1, 12)
                        if k == 3:
                            step_lo(1, 0, 1024, i, 1)
                for k in range(4):
                    lo(B + U_FF - 4, k)
                    if k == 0:
                        product(FF_STEPS, 1024, 2, B + U_FF - 4)
                    if k == 2:
                        step_lo(FF_STEPS, 0, 1024)
                for k in range(AHEAD):
                    lo(BASE_MIX[1], k)
                add_acc(2, B + U_FF)

            def build_g(p, e):
                for t in range(TT):
                    ins = dve.tensor_scalar(g_t[:, t, :], cst[:, C_IOTA + P * p:C_IOTA + P * p + P],
                                            pos[:, t, bass.ds(e, 1)] if not isinstance(e, int) else pos[:, t, e:e + 1],
                                            mask[:, t, bass.ds(e, 1)] if not isinstance(e, int) else mask[:, t, e:e + 1],
                                            ALU.is_equal, ALU.mult)
                ins.then_inc(g_ok, 1)

            def experts(p):
                B = BASE_MOE + p * E * U_EX

                def product_rows(s, e):
                    dve.wait_ge(unit_used, e * U_EX + (B + (8, 16, 28)[s]))
                    dve.wait_ge(silu_ok, e * FE_STEPS + ff_count(p, 0, s))
                    dve.wait_ge(prod_ok, e * FE_STEPS + (ff_count(p, 0, s) - 1))
                    if s or p:
                        dve.wait_ge(at_ps, e * FE_STEPS + (at_count(p, s) - 1))
                    dve.tensor_tensor(prod_t[:, 0:512], ps[:, 2 * (s % 2) + 1, :], silu_t[:, 0:512],
                                      ALU.mult).then_inc(prod_ok, 1)

                def product_lo(s, e):
                    dve.wait_ge(ah_ok, e * FE_STEPS + ff_count(p, 0, s))
                    o = 2048 + 512 * (s % 2)
                    dve.tensor_tensor(ylf[:, o:o + 512], ps[:, 2 * (s % 2), :], yhf[:, o:o + 512].bitcast(F32),
                                      ALU.subtract).then_inc(al_ok, 1)

                def gather_rows(n, e):
                    dve.wait_ge(gr_ps, e * 2 + (2 * n + 2))
                    dve.tensor_copy(xrow[:, 512:1024], ps[:, 7, :]).then_inc(xr_d, 1)

                def gather_lo(n, e):
                    for b in range(2):
                        dve.wait_ge(xgh_ok, e * 2 + (2 * n + b + 1))
                        dve.tensor_tensor(xg_l[:, 512 * b:512 * b + 512], ps[:, 6 + b, :],
                                          xg_h[:, 512 * b:512 * b + 512].bitcast(F32), ALU.subtract).then_inc(xgl_ok, 1)

                def rows_lo(n, e):
                    for b in range(2):
                        dve.wait_ge(ysh_ok, e * 2 + (2 * (n - 1) + b + 1))
                        dve.scalar_tensor_tensor(out=ys_l[:, 512 * b:512 * b + 512], in0=ps[:, 4 + b, :], scalar=slot_w,
                                                 in1=ys_h[:, 512 * b:512 * b + 512].bitcast(F32), op0=ALU.mult,
                                                 op1=ALU.subtract).then_inc(ysl_ok, 1)

                def scatter_add(n, e, qs=range(4)):
                    for q in qs:
                        t, half = q // 2, q % 2
                        dve.wait_ge(sc_ps, e * 4 + (4 * (n - 1) + q + 1))
                        dve.tensor_tensor(h[:, t, 512 * half:512 * half + 512], ps[:, (6, 7, 4, 5)[q], :],
                                          h[:, t, 512 * half:512 * half + 512], ALU.add).then_inc(sc_add, 1)

                if p == 0:
                    for b in range(2):
                        dve.wait_ge(xt_ps, 4 * 3 + 2 + b + 1)
                        dve.tensor_copy(xt_full[:, 1024 + 512 * b:1024 + 512 * b + 512], ps[:, 6 + b, :])\
                            .then_inc(xt_d, 1)
                    link(dve.memset(gt_t[:, :, :].bitcast(F32), 0.0))
                    dve.wait_ge(hnh_ok, 2)
                    dve.tensor_tensor(ylf[:, D:2 * D], gflat[:, D:2 * D], yhf[:, D:2 * D].bitcast(F32),
                                      ALU.subtract).then_inc(hnl_dve, 1)
                    route()
                build_g(p, 0)
                if p == 0:
                    route_weights()
                dve.memset(slot_w, 0.0).then_inc(slot_zero, 1)
                gather_rows((E + 1) * p, 0)
                gather_lo((E + 1) * p, 0)
                with dve.Fori(0, E) as e:
                    for k in range(AHEAD):
                        lo(B, k, e, U_EX)
                    rows_lo((E + 1) * p + 1, e)
                    for k in range(AHEAD, U_EX):
                        lo(B, k, e, U_EX)
                        if k == 11:
                            product_rows(0, e)
                        if k in (12, 13):
                            scatter_add((E + 1) * p + 1, e, (range(0, 2), range(2, 4))[k - 12])
                        if k == 14:
                            product_lo(0, e)
                        if k == 19:
                            product_rows(1, e)
                        if k == 23:
                            dve.wait_ge(gt_ps, e + (E * p + 1))
                            build_g(p, e + 1)
                            product_lo(1, e)
                        if k == 28:
                            gather_rows((E + 1) * p + 1, e)
                        if k == 31:
                            product_rows(2, e)
                            gather_lo((E + 1) * p + 1, e)
                        if k == 32:
                            product_lo(2, e)
                rows_lo((E + 1) * (p + 1), 0)
                scatter_add((E + 1) * (p + 1), 0)
                dve.wait_ge(sc_add, 4 * (E + 1) * (p + 1))

            def route():
                link(dve.memset(small[:, 80:152], 0.0))
                dve.wait_ge(lg_ps, 1)
                dve.tensor_copy(p_t[0:E, 0, :], ps[0:E, 0, 0:SEQ]).then_inc(lg_row, 1)
                dve.wait_ge(lg_t, 1)
                link(dve.tensor_copy(logit, ps[:, 1, 0:TT * E].rearrange("p (t e) -> p t e", t=TT)))
                for t in range(TT):
                    i = dve.max(top8[:, t, :], logit[:, t, :])
                link(i)
                for t in range(TT):
                    i = dve.max_index(idx[:, t, :], top8[:, t, :], logit[:, t, :])
                link(i)
                link(dve.tensor_copy(idxf[:, :, 0:2], idx[:, :, 0:2]))
                for t in range(TT):
                    for j, oh in enumerate((oh1, oh2)):
                        i = dve.tensor_scalar(oh[:, t, :], cst[:, C_I8:C_I8 + E], idxf[:, t, j:j + 1], None,
                                              ALU.is_equal)
                link(i)
                dve.tensor_tensor(mask[:, :, 0:E], oh1, oh2, ALU.add).then_inc(mask_ok, 1)
                dve.tensor_tensor(wtop[:, :, 1:2], top8[:, :, 1:2], top8[:, :, 0:1], ALU.subtract).then_inc(lg_d, 1)
                dve.wait_ge(pos_ps, 1)
                link(dve.tensor_copy(pos[:, :, 0:E], ps[:, 1, 64:64 + TT * E].rearrange("p (t e) -> p t e", t=TT)))

            def route_weights():
                dve.wait_ge(w2_ok, 1)
                link(dve.tensor_scalar(wtop[:, :, 3:4], wtop[:, :, 2:3], 1.0, None, ALU.add))
                link(dve.reciprocal(wtop[:, :, 4:5], wtop[:, :, 3:4]))
                link(dve.tensor_tensor(wtop[:, :, 5:6], wtop[:, :, 4:5], wtop[:, :, 2:3], ALU.mult))
                for t in range(TT):
                    i = dve.tensor_scalar(comb[:, t, 0:E], oh1[:, t, :], wtop[:, t, 4:5], None, ALU.mult)
                link(i)
                for t in range(TT):
                    i = dve.scalar_tensor_tensor(out=comb[:, t, 0:E], in0=oh2[:, t, :], scalar=wtop[:, t, 5:6],
                                                 in1=comb[:, t, 0:E], op0=ALU.mult, op1=ALU.add)
                i.then_inc(comb_ok, 1)
                dve.wait_ge(cnt_ps, 1)
                link(dve.tensor_reduce(cmax, ps[:, 3, 0:E], AX_X, ALU.max))
                dve.tensor_copy(cnt_i[:, 0:1], cmax).then_inc(cnt_ok, 1)

            dve.memset(eps_t[:, :], EPS).then_inc(eps_ok, 1)
            mixer(0)
            dense()
            mixer(1)
            norm(3)
            experts(0)
            dve.wait_ge(cnt_ok, 1)
            most = dve.value_load(cnt_i[0:1, 0:1], min_val=0, max_val=SEQ)
            with dve.If(most > FIRST_SLOTS):
                experts(1)
            dve.memset(cmax, 0.0).then_inc(h_ready, TT)
            norm(4)

        @block.tensor
        def _(pe):
            mm = pe.matmul

            def mm3(dst, ah, al, bh, bl, first, last):
                mm(dst, ah, bh, start=first, stop=False, skip_group_check=True)
                mm(dst, ah, bl, start=False, stop=False, skip_group_check=True)
                return mm(dst, al, bh, start=False, stop=last, skip_group_check=True)

            def split(base, k, i=0, per=0):
                u = base + k
                pe.wait_ge(lo_dve, i * per + (u + 1))
                pe.wait_ge(lo_pool, i * per + (u + 1))
                return w_hi[:, u % RH, :], w_lo[:, u % RH, :]

            def unit_columns(base, k, r, banks, xs, width, i=0, per=0, last=None):
                wh, wl = split(base, k, i, per)
                for kk in range(2):
                    for m in range(4):
                        at = width * m
                        dst = ps[:, banks + at // 512, at % 512:at % 512 + width]
                        c = 2 * r + kk
                        o = 512 * kk + P * m
                        ins = mm3(dst, wh[:, o:o + P], wl[:, o:o + P], xs[0][:, width * c:width * c + width],
                                  xs[1][:, width * c:width * c + width],
                                  first=(c == 0 and at % 512 == 0), last=(last == c))
                ins.then_inc(unit_used, 1)
                return ins

            def unit_tokens(base, k, r, banks, i=0, per=0):
                wh, wl = split(base, k, i, per)
                for kk in range(2):
                    for t in range(TT):
                        c = 2 * r + kk
                        ins = mm3(ps[:, banks + t, :], xh[:, c, P * t:P * t + P], xl[:, c, P * t:P * t + P],
                                  wh[:, 512 * kk:512 * kk + 512], wl[:, 512 * kk:512 * kk + 512],
                                  first=(c == 0), last=(c == KC - 1))
                ins.then_inc(unit_used, 1)

            def unit_wide(base, k, a_h, a_l, tiles, first, last, i=0, per=0):
                wh, wl = split(base, k, i, per)
                for t in range(tiles):
                    for half in range(2):
                        ins = mm3(ps[:, 4 + 2 * t + half, :], a_h[:, P * t:P * t + P], a_l[:, P * t:P * t + P],
                                  wh[:, 512 * half:512 * half + 512], wl[:, 512 * half:512 * half + 512],
                                  first=first, last=last)
                    if last and t < tiles - 1:
                        ins.then_inc(acc_first, 1)
                ins.then_inc(unit_used, 1)

            def norm(n):
                for t in range(TT):
                    for c in range(KC):
                        if c % (KC // 2) == 0:
                            pe.wait_ge(normed, 2 * (TT * n + t) + c // (KC // 2) + 1)
                        at = SEQ * (c % 2) + P * t
                        ins = pe.transpose(ps[:, 4 + c // 2, at:at + P], hn[:, t, P * c:P * c + P], ident)
                        if t == TT - 1 and c % 2:
                            ins.then_inc(xt_ps, 1)

            def mixer(l):
                B = BASE_MIX[l]
                norm(2 * l)
                for k in range(U_MIX):
                    if l == 0 and k == 1:
                        pe.wait_ge(vec_in, 16 * 6)
                        pe.transpose(ps[:, 2, 0:2 * NB], rows_in[0:2 * NB, 0, :], ident[0:2 * NB, 0:2 * NB])
                        n = N_COL - 2 * NB
                        pe.transpose(ps[:, 3, 0:n], rows_in[0:n, 1, :], ident[0:n, 0:n]).then_inc(vec_t, 1)
                    if l == 0 and k == 4:
                        pe.wait_ge(col_ok, 1)
                        pe.wait_ge(const_in, 16)
                    if k == AT_F1:
                        pe.wait_ge(evac_d, evacs(DVE_EVACS, l, 0))
                        pe.wait_ge(xl_ok, 8 * l + 4)
                        for m in range(BC):
                            for t in range(TT):
                                at = C_DFT + 2 * SEQ * t
                                ins = mm(ps[:, 4 + m, :], uf_t[:, BR * t + P * m:BR * t + P * m + P],
                                         cst[:, at:at + 2 * SEQ], start=(t == 0), stop=(t == TT - 1))
                        ins.then_inc(f1_ps, 1)
                    if k == AT_F2:
                        pe.wait_ge(ut_a, l + 1)
                        pe.wait_ge(ut_d, l + 1)
                        for m in range(BC):
                            for s in range(2):
                                src = lru[:, m // 2, 512 * (m % 2) + SEQ * s:512 * (m % 2) + SEQ * s + SEQ]
                                ins = mm(ps[:, 4 + m // 2, SEQ * (m % 2):SEQ * (m % 2) + SEQ],
                                         cst[:, C_CC + P * s:C_CC + P * s + P], src, start=(s == 0), stop=(s == 1))
                        ins.then_inc(f2_ps, 1)
                    for d, at in ((0, AT_LF), (1, AT_LB)):
                        if k == at:
                            if d:
                                pe.wait_ge(lru_tanh, 2 * (2 * l + 1))
                            else:
                                pe.wait_ge(yb_l, l + 1)
                                pe.wait_ge(conv_ok, l + 1)
                                pe.wait_ge(wlru_in, 16 * 8 * (l + 1))
                            for g in range(2):
                                for m in range(BC):
                                    for hh in range(2):
                                        q = slice(HD * hh, HD * hh + HD)
                                        ins = mm(ps[q, 4 + 2 * g + m // 2, SEQ * (m % 2):SEQ * (m % 2) + SEQ],
                                                 wlru[q, d, g, m, :], conv_t[q, m, :], start=True, stop=True)
                            ins.then_inc(lru_ps, 1)
                    j = k - AT_ATT
                    if 0 <= j < NA:
                        hp, t, hh = UNITS_ATT[j]
                        if j == 0:
                            pe.wait_ge(evac_a, evacs(ACT_EVACS, l, 3))
                            pe.wait_ge(evac_d, evacs(DVE_EVACS, l, 4))
                            pe.wait_ge(lru_tanh, 4 * (l + 1))
                        else:
                            pe.wait_ge(s_max, NA * l + j)
                        q = slice(HD * hh, HD * hh + HD)
                        mm(ps[:, 4, 0:SEQ], q_t[q, hp, P * t:P * t + P], k_t[q, hp, :],
                           start=True, stop=True).then_inc(s_ps, 1)
                    if 2 <= j < NA + 2:
                        pe.wait_ge(p_norm, NA * l + j - 1)
                        if j > 2:
                            pe.wait_ge(pt_ok, NA * l + j - 2)
                        for kt in range(TT):
                            ins = pe.transpose(ps[:, 5, P * kt:P * kt + P], p_t[:, j % 2, P * kt:P * kt + P], ident)
                        ins.then_inc(pt_ps, 1)
                    if 3 <= j < NA + 3:
                        hp, t, hh = UNITS_ATT[j - 3]
                        pe.wait_ge(pt_ok, NA * l + j - 2)
                        if hp >= 2:
                            pe.wait_ge(ya_l, 4 * l + hp - 1)
                        hd = 2 * hp + hh
                        for kt in range(TT):
                            ins = mm(ps[HD * hh:HD * hh + HD, 6 + hp % 2, P * t:P * t + P],
                                     v_t[:, kt, HD * hd:HD * hd + HD], pt_t[:, (j - 1) % 2, P * kt:P * kt + P],
                                     start=(kt == 0), stop=(kt == TT - 1))
                        ins.then_inc(av_ps, 1)
                    if k < U_IN:
                        n, r = k // 4, k % 4
                        if r == 0:
                            if n >= 2:
                                pe.wait_ge(evac_a, evacs(ACT_EVACS, l, n - 2))
                                pe.wait_ge(evac_d, evacs(DVE_EVACS, l, n - 2))
                            elif l and n == 0:
                                pe.wait_ge(prod_ok, FF_STEPS)
                        if n == 0:
                            pe.wait_ge(xl_ok, 8 * l + r + 1)
                        if GROUPS[n] in (UF, V):
                            unit_tokens(B, k, r, 2 * (n % 2))
                        else:
                            unit_columns(B, k, r, 2 * (n % 2), (xhf, xlf), SEQ, last=KC - 1)
                    elif k < U_IN + U_BR:
                        nb, r = (k - U_IN) // 2, (k - U_IN) % 2
                        dg, br = BRANCHES[nb]
                        n = len(GROUPS) + nb
                        if r == 0:
                            pe.wait_ge(evac_a, evacs(ACT_EVACS, l, n - 2))
                            pe.wait_ge(evac_d, evacs(DVE_EVACS, l, n - 2))
                            if dg == 0:
                                {1: lambda: pe.wait_ge(yb_l, l + 1), 2: lambda: pe.wait_ge(yc_l, l + 1),
                                 0: lambda: pe.wait_ge(ya_l, 4 * l + 4)}[br]()
                        unit_columns(B, k, r, 2 * (n % 2), (yhf[:, 1024 * br:1024 * br + 1024], ylf[:, 1024 * br:1024 * br + 1024]),
                                     SEQ, last=BC - 1)
                    else:
                        r = k - U_IN - U_BR
                        if r % 2 == 0:
                            pe.wait_ge(ml_ok, 4 * l + r // 2 + 1)
                        unit_wide(B, k, xh[:, r, :], xl[:, r, :], TT, r == 0, r == U_OUT - 1)

            def dense():
                B = BASE_FF
                norm(1)

                def gate_up(B, n, i=0, per=0):
                    for k in range(8):
                        if k < 4 and n == 1:
                            pe.wait_ge(xl_ok, 4 + k + 1)
                        if n > 1 and k == 0:
                            pe.wait_ge(silu_ok, i + (n - 1))
                        if n > 1 and k == 4:
                            pe.wait_ge(prod_ok, i + (n - 1))
                        unit_columns(B, k, k % 4, 2 * (k // 4), (xhf, xlf), SEQ, i, per, last=KC - 1)

                def down(B, n, first, last, i=0, per=0):
                    pe.wait_ge(al_ok, i + n)
                    for k in range(4):
                        unit_wide(B, k, yh[:, k, :], yl[:, k, :], TT, first and k == 0, last and k == 3, i, per)

                gate_up(B, 1)
                gate_up(B + 8, 2)
                down(B + 16, 1, True, False)
                with pe.Fori(0, FF_STEPS - 2) as i:
                    gate_up(B + 20, 3, i, 12)
                    down(B + 28, 2, False, False, i, 12)
                down(B + U_FF - 4, FF_STEPS, False, True)

            def gather(n, e):
                pe.wait_ge(g_ok, e + n)
                for half in range(2):
                    for t in range(TT):
                        o = D * t + 512 * half
                        mm(ps[:, 6 + half, :], g_t[:, t, :], yhf[:, o:o + 512], start=(t == 0), stop=False)
                        ins = mm(ps[:, 6 + half, :], g_t[:, t, :], ylf[:, o:o + 512], start=False, stop=(t == TT - 1))
                    ins.then_inc(gr_ps, 1)

            def turn_rows(n, e):
                pe.wait_ge(xr_a, e + n)
                pe.wait_ge(xr_d, e + n)
                for c in range(KC):
                    ins = pe.transpose(ps[:, 6 + c // 4, P * (c % 4):P * (c % 4) + P], xrow[:, P * c:P * c + P], ident)
                    if c % 4 == 3:
                        ins.then_inc(gth_ps, 1)

            def scatter(n, e):
                pe.wait_ge(ysl_ok, e * 2 + 2 * n)
                for q in range(4):
                    t, half = q // 2, q % 2
                    dst = ps[:, (6, 7, 4, 5)[q], :]
                    mm(dst, gt_t[:, t, :], ys_h[:, 512 * half:512 * half + 512], start=True, stop=False)
                    mm(dst, gt_t[:, t, :], ys_l[:, 512 * half:512 * half + 512], start=False,
                       stop=True).then_inc(sc_ps, 1)

            def route():
                pe.wait_ge(rw_in, 16)
                for c in range(KC):
                    if c % 2 == 0:
                        pe.wait_ge(xt_a if c < KC // 2 else xt_d, (c % (KC // 2)) // 2 + 1)
                    ins = mm(ps[0:E, 0, 0:SEQ], rw[:, c, :], xt_full[:, SEQ * c:SEQ * c + SEQ],
                             start=(c == 0), stop=(c == KC - 1))
                ins.then_inc(lg_ps, 1)
                pe.wait_ge(lg_row, 1)
                for t in range(TT):
                    ins = pe.transpose(ps[:, 1, E * t:E * t + E], p_t[0:E, 0, P * t:P * t + P], ident[0:E, 0:E])
                ins.then_inc(lg_t, 1)
                pe.wait_ge(mask_ok, 1)
                mm(ps[:, 1, 64:64 + E], tri, mask[:, 0, 0:E], start=True, stop=True)
                mm(ps[:, 1, 64 + E:64 + 2 * E], tri, mask[:, 1, 0:E], start=True, stop=False)
                mm(ps[:, 1, 64 + E:64 + 2 * E], ones, mask[:, 0, 0:E], start=False, stop=True).then_inc(pos_ps, 1)
                mm(ps[:, 3, 0:E], ones, mask[:, 0, 0:E], start=True, stop=False)
                mm(ps[:, 3, 0:E], ones, mask[:, 1, 0:E], start=False, stop=True).then_inc(cnt_ps, 1)

            def experts(p):
                B = BASE_MOE + p * E * U_EX
                n0 = (E + 1) * p
                if p == 0:
                    pe.wait_ge(hnl_dve, 1)
                    pe.wait_ge(hnl_pool, 1)
                gather(n0 + 1, 0)
                turn_rows(n0 + 1, 0)
                pe.wait_ge(comb_ok, 1)
                pe.wait_ge(cnt_ok, 1)

                def gate_up(k0, s, e, ks=range(8)):
                    for k in ks:
                        if s == 0 and k == 0:
                            pe.wait_ge(prod_ok, e * FE_STEPS + (ff_count(p, 0, 0) - 1))
                            pe.wait_ge(xgl_ok, e * 2 + 2 * (n0 + 1))
                        if s == 2 and k == 0:
                            pe.wait_ge(prod_ok, e * FE_STEPS + ff_count(p, 0, 0))
                        wh, wl = split(B, k0 + k, e, U_EX)
                        for kk in range(2):
                            c = 2 * (k % 4) + kk
                            ins = mm3(ps[:, 2 * (s % 2) + k // 4, :], xg_h[:, P * c:P * c + P], xg_l[:, P * c:P * c + P],
                                      wh[:, 512 * kk:512 * kk + 512], wl[:, 512 * kk:512 * kk + 512],
                                      first=(c == 0), last=(c == KC - 1))
                        ins.then_inc(unit_used, 1)

                def turn_product(s, e):
                    pe.wait_ge(prod_ok, e * FE_STEPS + ff_count(p, 0, s))
                    for m in range(4):
                        ins = pe.transpose(ps[:, 2 * (s % 2), P * m:P * m + P], prod_t[:, P * m:P * m + P], ident)
                    ins.then_inc(at_ps, 1)

                def down(k0, s, e, ks=range(4)):
                    pe.wait_ge(al_ok, e * FE_STEPS + ff_count(p, 0, s))
                    if s == 0:
                        pe.wait_ge(ysl_ok, e * 2 + 2 * (n0 + 1))
                    for k in ks:
                        o = 2048 + 512 * (s % 2) + P * k
                        unit_wide(B, k0 + k, yhf[:, o:o + P], ylf[:, o:o + P], 1, s == 0 and k == 0,
                                  s == FE_STEPS - 1 and k == 3, e, U_EX)

                with pe.Fori(0, E) as e:
                    gate_up(0, 0, e)
                    scatter(n0 + 1, e)
                    gate_up(8, 1, e, range(3))
                    turn_product(0, e)
                    gate_up(8, 1, e, range(3, 8))
                    pe.wait_ge(sc_add, e * 4 + 4 * (n0 + 1))
                    for t in range(TT):
                        pe.transpose(ps[:, 6, P * t:P * t + P], g_t[:, t, :].bitcast(F32), ident)
                    for t in range(TT):
                        ins = mm(ps[:, 6, 2 * P:2 * P + 1], g_t[:, t, :].bitcast(F32), comb[:, t, bass.ds(e, 1)],
                                 start=(t == 0), stop=(t == TT - 1))
                    ins.then_inc(gt_ps, 1)
                    down(16, 0, e)
                    turn_product(1, e)
                    gate_up(20, 2, e, range(5))
                    pe.wait_ge(gt_ok, e * 2 + 2 * (E * p + 1))
                    gather(n0 + 2, e)
                    gate_up(20, 2, e, range(5, 8))
                    turn_rows(n0 + 2, e)
                    down(28, 1, e, range(1))
                    turn_product(2, e)
                    down(28, 1, e, range(1, 4))
                    down(32, 2, e)
                scatter(n0 + E + 1, 0)

            pe.wait_ge(ident_in, 16)
            mixer(0)
            dense()
            mixer(1)
            norm(3)
            route()
            experts(0)
            pe.wait_ge(cnt_ok, 1)
            most = pe.value_load(cnt_i[0:1, 0:1], min_val=0, max_val=SEQ)
            with pe.If(most > FIRST_SLOTS):
                experts(1)


_INS = ["x", "norm_mix_g", "w_in", "b_in", "na_rpb", "conv_w", "conv_b", "lru_wa", "lru_ba", "lru_wx", "lru_bx",
        "lru_lambda", "w_branch", "w_out", "norm_ffn_g", "ffn_w_gu", "ffn_w_down", "router_w", "moe_w_gu",
        "moe_w_down", "final_g"]


def kernel(**inputs):
    import concourse.bacc as _bacc
    from concourse.bass_utils import run_bass_kernel_spmd as _run

    arrays = {name: np.asarray(inputs[name]) for name in _INS}
    rpb = np.zeros(arrays["na_rpb"].shape[:3] + (P,), np.float32)
    rpb[..., GRID_W - KW:GRID_W + KW - 1] = arrays["na_rpb"][..., ::-1]
    arrays["na_rpb"] = rpb
    arrays["consts"] = constants()
    nc = _bacc.Bacc("TRN2", target_bir_lowering=False, num_devices=1)
    feeds, args = {}, []
    for name, a in arrays.items():
        a = np.ascontiguousarray(a)
        feeds[f"in_{name}_dram"] = a
        args.append(nc.dram_tensor(f"in_{name}_dram", a.shape, mybir.dt.from_np(a.dtype), kind="ExternalInput").ap())
    args.append(nc.dram_tensor("out_0_dram", (1, SEQ, D), F32, kind="ExternalOutput").ap())
    build(nc, *args)
    r = _run(nc, [feeds], core_ids=[0])
    return r.results[0]["out_0_dram"]
```

```python
import math
from contextlib import ExitStack

import numpy as np

import concourse.bass as bass
from concourse import mybir

F32 = mybir.dt.float32
F32R = mybir.dt.float32r
U32 = mybir.dt.uint32
I32 = mybir.dt.int32
ALU = mybir.AluOpType
ACT = mybir.ActivationFunctionType
AX_X = mybir.AxisListType.X
GELU_C = math.sqrt(2 / math.pi)

P = 128
SEQ, D = 256, 1024
TT = SEQ // P
KC = D // P
GRID_W = 64
ROWS = SEQ // GRID_W
HEADS, HD = 8, 64
KH_MAX, KW = 8, 16
BR = 512
BC = BR // P
IN_COLS = 3 * BR + BR + 2 * BR + 3 * D
D_FF = 3 * D
E, FE = 8, D_FF // 2
SCALE = HD ** -0.5
EPS = 1e-6
NEG = -1e30
BT_SLOTS = ROWS + 2

UNIT = 1024
RAW = 6
RAW_MOE = 18
RH = 4
CUT, CUT_MOE = 512, 704
AHEAD = RH - 1

UF, UX, Q, K, V, UG = 3, 4, 0, 1, 2, 5
GROUPS = [UF, UX, Q, K, V, UG] + list(range(6, 12))
GATE0 = 6
U_IN = 4 * len(GROUPS)
BRANCHES = [(dg, k) for dg in range(2) for k in (1, 2, 0)]
U_BR = 2 * len(BRANCHES)
U_OUT = KC
U_MIX = U_IN + U_BR + U_OUT
FF_STEPS = D_FF // 512
U_FF = 12 * FF_STEPS
FE_STEPS = FE // 512
U_EX = 12 * FE_STEPS
BASE_MIX = [0, U_MIX + U_FF]
BASE_FF = U_MIX
BASE_MOE = 2 * U_MIX + U_FF

AT_F1, AT_F2, AT_LF, AT_LB, AT_GELU, AT_ATT = 8, 12, 16, 25, 34, 28
AT_CONV = 9
AT_MASK = (14, 16, 18, 20)
UNITS_ATT = [(hp, t) for hp in range(HEADS // 2) for t in range(TT)]
NA = len(UNITS_ATT)

C_ID, C_TRI, C_ONE, C_IOTA, C_CC, C_MASK, C_DFT, C_I8 = 0, 128, 256, 384, 640, 896, 960, 1472
C_COLS = 1480
FIRST_SLOTS = 128


def constants():
    c = np.zeros((P, C_COLS), np.float32)
    i = np.arange(P)
    c[:, C_ID:C_ID + P] = np.eye(P)
    c[:, C_TRI:C_TRI + P] = i[:, None] < i[None, :]
    c[:, C_ONE:C_ONE + P] = 1.0
    c[:, C_IOTA:C_IOTA + P] = np.where(i < FIRST_SLOTS, i, -1)
    c[:, C_IOTA + P:C_IOTA + 2 * P] = FIRST_SLOTS + i
    ang = 2 * np.pi * ((i[:, None] * i[None, :]) % HD) / HD
    same = (i[:, None] // HD) == (i[None, :] // HD)
    c[:, C_CC:C_CC + P] = np.cos(ang) * same
    c[:, C_CC + P:C_CC + 2 * P] = -np.sin(ang) * same
    col = i % GRID_W
    start = np.clip(col - KW // 2, 0, GRID_W - KW)
    kc = GRID_W - 1 - np.arange(GRID_W)
    inside = (kc[None, :] >= start[:, None]) & (kc[None, :] < start[:, None] + KW)
    c[:, C_MASK:C_MASK + GRID_W] = np.where(inside, 0.0, NEG)
    s = np.arange(P + 1)
    for t in range(TT):
        a = 2 * np.pi * (((t * P + i)[:, None] * s[None, :]) % SEQ) / SEQ
        at = C_DFT + t * SEQ
        c[:, at:at + P + 1] = np.cos(a) / math.sqrt(SEQ * HD)
        c[:, at + P + 1:at + SEQ] = np.sin(a)[:, 1:P] / math.sqrt(SEQ * HD)
    c[:, C_I8:C_I8 + 8] = np.arange(8)
    return c


def build(nc, x, norm_mix_g, w_in, b_in, rpb, conv_w, conv_b, lru_wa, lru_ba, lru_wx, lru_bx,
          lru_lambda, w_branch, w_out, norm_ffn_g, ffn_w_gu, ffn_w_down, router_w, moe_w_gu,
          moe_w_down, final_g, consts, out):
    with ExitStack() as ctx:
        def sb(name, shape, dt=F32):
            return ctx.enter_context(nc.sbuf_tensor(name, shape, dt))

        def sem(name):
            return ctx.enter_context(nc.semaphore(name))

        raw = sb("raw", [P, RAW, UNIT])
        w_hi = sb("w_hi", [P, RH, UNIT], F32R)
        w_lo = sb("w_lo", [P, RH, UNIT], F32R)
        h = sb("h", [P, TT, D])
        xh = sb("xh", [P, KC, SEQ], F32R)
        xl = sb("xl", [P, KC, SEQ], F32R)
        yh = sb("yh", [P, 3 * BC, SEQ], F32R)
        yl = sb("yl", [P, 3 * BC, SEQ], F32R)
        gates = sb("gates", [P, 3 * KC, SEQ])
        gflat = gates[:, :, :].rearrange("p c s -> p (c s)")
        hn = gflat[:, 0:TT * D].rearrange("p (t d) -> p t d", t=TT)
        junk = gflat[:, TT * D:2 * TT * D].rearrange("p (t d) -> p t d", t=TT)
        rows_in = gflat[:, 5 * D:5 * D + 2 * P].rearrange("p (a b) -> p a b", a=2)
        xrow = gflat[:, 2 * D:3 * D]
        xt_full = gflat[:, 4 * D:6 * D]
        silu_t = gflat[:, 3 * D:4 * D]
        prod_t = gflat[:, 4 * D:5 * D]
        W = BC * SEQ
        N_BIAS, N_UX = HEADS * BT_SLOTS * GRID_W, BC * (SEQ + 4)
        mix = sb("mix", [P, N_BIAS + 9 * W + N_UX])
        bias_t = mix[:, 0:N_BIAS].rearrange("p (s c) -> p s c", c=GRID_W)
        q_t, k_t, v_t, uf_t, ug_t, conv_t = (mix[:, N_BIAS + W * i:N_BIAS + W * i + W] for i in range(6))
        q_t, k_t, conv_t = (a.rearrange("p (c s) -> p c s", c=BC) for a in (q_t, k_t, conv_t))
        v_t = v_t.rearrange("p (t n) -> p t n", t=TT)
        lru = mix[:, N_BIAS + 6 * W:N_BIAS + 9 * W].rearrange("p (a n) -> p a n", a=3)
        ux_t = mix[:, N_BIAS + 9 * W:N_BIAS + 9 * W + N_UX].rearrange("p (c s) -> p c s", c=BC)
        row = sb("row", [P, D])
        p_t = sb("p_t", [P, 2, 2, SEQ])
        pt_t = sb("pt_t", [P, 2, SEQ])
        cst = sb("cst", [P, C_COLS])
        col = sb("col", [P, 192])
        col2 = sb("col2", [P, 120])
        small = sb("small", [P, 200])
        wlru = sb("wlru", [P, 2, 2, BC, HD])
        rw = sb("rw", [P, KC, E])
        g_t = sb("g_t", [P, TT, P], F32R)
        gt_t = sb("gt_t", [P, TT, P], F32R)
        idx = sb("idx", [P, TT, 8], U32)
        cnt_i = sb("cnt_i", [P, 2], I32)
        eps_t = sb("eps_t", [P, 1])
        ps = ctx.enter_context(nc.psum_tensor("ps", [P, 8, 512], F32))

        ux_in = ux_t[:, :, 2:2 + SEQ]
        cflat = conv_t[:, :, :].rearrange("p c s -> p (c s)")
        ident = cst[:, C_ID:C_ID + P]
        tri = cst[:, C_TRI:C_TRI + P]
        ones = cst[:, C_ONE:C_ONE + P]
        NB = IN_COLS // P
        O_CW = 2 * NB
        O_CB = O_CW + 2 * 4 * BC
        O_BA = O_CB + 2 * BC
        O_BX = O_BA + 4 * BC
        O_LAM = O_BX + 4 * BC
        N_COL = O_LAM + 4 * BC
        O_SP, O_NSP, O_HBA, O_HBX, O_BQ, O_GB = 0, 16, 32, 48, 64, 72
        lam_w = small[:, 96:192].rearrange("p (a b) -> p a b", a=6)
        ss, rms, rinv = small[:, 0:2], small[:, 2:4], small[:, 4:6]
        table_in = small[:, 6:7]
        smax, nmax, rsum, rrec = (small[:, 184 + 4 * i:188 + 4 * i].rearrange("p (b h) -> p b h", b=2) for i in range(4))
        logit = small[:, 16:32].rearrange("p (t e) -> p t e", t=TT)
        top8 = small[:, 32:48].rearrange("p (t e) -> p t e", t=TT)
        oh1 = small[:, 48:64].rearrange("p (t e) -> p t e", t=TT)
        oh2 = small[:, 64:80].rearrange("p (t e) -> p t e", t=TT)
        mask = small[:, 80:104].rearrange("p (t e) -> p t e", t=TT)
        comb = small[:, 104:128].rearrange("p (t e) -> p t e", t=TT)
        pos = small[:, 128:152].rearrange("p (t e) -> p t e", t=TT)
        wtop = small[:, 152:168].rearrange("p (t e) -> p t e", t=TT)
        cnt = small[:, 168:176]
        cmax = small[:, 176:177]
        slot_w = small[:, 177:178]
        idxf = small[:, 180:184].rearrange("p (t e) -> p t e", t=TT)
        xg_h = xh[:, 0:4, :].rearrange("p c s -> p (c s)")
        xg_l = xl[:, 0:4, :].rearrange("p c s -> p (c s)")
        ys_h = xh[:, 4:8, :].rearrange("p c s -> p (c s)")
        ys_l = xl[:, 4:8, :].rearrange("p c s -> p (c s)")
        yhf = yh[:, :, :].rearrange("p c s -> p (c s)")
        ylf = yl[:, :, :].rearrange("p c s -> p (c s)")
        xhf = xh[:, :, :].rearrange("p c s -> p (c s)")
        xlf = xl[:, :, :].rearrange("p c s -> p (c s)")

        raw_full = [sem(f"raw_full{i}") for i in range(RAW)]
        mix_full = [sem(f"mix_full{i}") for i in range(RAW_MOE - RAW)]
        hi_done, lo_dve, lo_pool, unit_used = sem("hi_done"), sem("lo_dve"), sem("lo_pool"), sem("unit_used")
        ident_in, const_in, vec_in, rw_in = sem("ident_in"), sem("const_in"), sem("vec_in"), sem("rw_in")
        x_in = [sem(f"x_in{t}") for t in range(TT)]
        bias_in, wlru_in, row_in = sem("bias_in"), sem("wlru_in"), sem("row_in")
        vec_t, col_ok, lam_act, col2_ok, zeroed = sem("vec_t"), sem("col_ok"), sem("lam_act"), sem("col2_ok"), sem("zeroed")
        eps_ok, bias_ok = sem("eps_ok"), sem("bias_ok")
        h_ready, squares, rms_ok, normed = sem("h_ready"), sem("squares"), sem("rms_ok"), sem("normed")
        xt_ps, xh_ok, xl_ok, acc_first = sem("xt_ps"), sem("xh_ok"), sem("xl_ok"), sem("acc_first")
        evac_a, evac_d = sem("evac_a"), sem("evac_d")
        f1_ps, ut_a, ut_d, f2_ps, yb_full, yb_h, yb_l = sem("f1_ps"), sem("ut_a"), sem("ut_d"), sem("f2_ps"), sem("yb_full"), sem("yb_h"), sem("yb_l")
        conv_ok, lru_ps, lru_tanh, lru_dec, mult_in, mult_ok, scanned = (
            sem("conv_ok"), sem("lru_ps"), sem("lru_tanh"), sem("lru_dec"), sem("mult_in"), sem("mult_ok"), sem("scanned"))
        gelu_in, gelu_t, yc_ok, yc_h, yc_l = sem("gelu_in"), sem("gelu_t"), sem("yc_ok"), sem("yc_h"), sem("yc_l")
        s_ps, s_max, p_exp, p_norm, pt_ps, pt_ok, av_ps, ya_h, ya_l = (
            sem("s_ps"), sem("s_max"), sem("p_exp"), sem("p_norm"), sem("pt_ps"), sem("pt_ok"), sem("av_ps"), sem("ya_h"), sem("ya_l"))
        merged, mh_ok, ml_ok = sem("merged"), sem("mh_ok"), sem("ml_ok")
        silu_ok, prod_ok, ah_ok, al_ok, at_ps = sem("silu_ok"), sem("prod_ok"), sem("ah_ok"), sem("al_ok"), sem("at_ps")
        hnh_ok, hnl_dve, hnl_pool, xt_a, xt_d, lg_ps, lg_row, lg_t, lg_d, w2_ok, mask_ok, comb_ok, pos_ps, cnt_ps, cnt_ok = (
            sem("hnh_ok"), sem("hnl_dve"), sem("hnl_pool"), sem("xt_a"), sem("xt_d"), sem("lg_ps"), sem("lg_row"), sem("lg_t"), sem("lg_d"), sem("w2_ok"), sem("mask_ok"), sem("comb_ok"), sem("pos_ps"),
            sem("cnt_ps"), sem("cnt_ok"))
        g_ok, gr_ps, xr_a, xr_d, gth_ps, xgh_ok, xgl_ok, gt_ps, gt_ok, slot_zero, ysh_ok, ysl_ok, sc_ps, sc_add = (
            sem("g_ok"), sem("gr_ps"), sem("xr_a"), sem("xr_d"), sem("gth_ps"), sem("xgh_ok"), sem("xgl_ok"), sem("gt_ps"), sem("gt_ok"), sem("slot_zero"),
            sem("ysh_ok"), sem("ysl_ok"), sem("sc_ps"), sem("sc_add"))
        out_ok, stored = sem("out_ok"), sem("stored")
        dve_link, act_link = sem("dve_link"), sem("act_link")

        ACT_EVACS = [g not in (UF, V) for g in GROUPS] + [False] * len(BRANCHES)
        DVE_EVACS = [g < GATE0 for g in GROUPS] + [True] * len(BRANCHES)

        def group_end(l, n):
            return BASE_MIX[l] + (4 * (n + 1) if n < len(GROUPS) else U_IN + 2 * (n + 1 - len(GROUPS)))

        def evacs(which, l, n):
            return l * sum(which) + sum(which[:n + 1])

        def ff_count(p, e, s):
            return 2 * FF_STEPS + E * FE_STEPS * p + FE_STEPS * e + s + 1

        def at_count(p, s):
            return E * FE_STEPS * p + s + 1

        def place(u):
            if u < BASE_MOE:
                return raw[:, u % RAW, :], raw_full[u % RAW], 16 * (u // RAW + 1)
            turn, j = (u - BASE_MOE) // RAW_MOE, (u - BASE_MOE) % RAW_MOE
            if j < RAW:
                return raw[:, (BASE_MOE + j) % RAW, :], raw_full[(BASE_MOE + j) % RAW], 16 * ((BASE_MOE + j) // RAW + turn + 1)
            return mix[:, UNIT * (j - RAW):UNIT * (j - RAW + 1)], mix_full[j - RAW], 16 * (turn + 1)

        block = ctx.enter_context(nc.Block())

        @block.sync
        def _(sp):
            def load(base, k, src, i=0, per=0):
                u = base + k
                ring = RAW_MOE if u >= BASE_MOE else RAW
                dst, arrived, _ = place(u)
                if u >= ring:
                    sp.wait_ge(lo_dve, i * per + (u - ring + 1))
                    sp.wait_ge(lo_pool, i * per + (u - ring + 1))
                sp.dma_start(dst.rearrange("p (k n) -> p k n", k=src.shape[1]), src).then_inc(arrived, 16)

            def square(w, r, c):
                return w[256 * r:256 * r + 256, 512 * c:512 * c + 512].rearrange("(k p) n -> p k n", p=P)

            def wide(w, r):
                return w[P * r:P * r + P, :].rearrange("(k p) n -> p k n", p=P)

            def load_tables(l, k):
                if 0 <= k < 4:
                    g, hh = k // 2, k % 2
                    w = (lru_wa, lru_wx)[g]
                    for d in range(2):
                        sp.dma_start(wlru[hh * HD:(hh + 1) * HD, d, g, :, :],
                                     w[l, d, hh::2, :, :].rearrange("m c o -> c m o")).then_inc(wlru_in, 16)
                elif 4 <= k < 4 + HEADS:
                    hd = k - 4
                    for r in range(2):
                        src = bass.AP(rpb.tensor, ((l * HEADS + hd) * (2 * KH_MAX - 1) + KH_MAX - ROWS + 1 - r) * P,
                                      [[1, GRID_W], [P, BT_SLOTS], [1, GRID_W]])
                        sp.dma_start(bias_t[r * GRID_W:(r + 1) * GRID_W, hd * BT_SLOTS:(hd + 1) * BT_SLOTS, :],
                                     src).then_inc(bias_in, 16)

            def load_vectors():
                sp.dma_start(rows_in[0:2 * NB, 0, :], b_in.rearrange("l (j p) -> (l j) p", p=P)).then_inc(vec_in, 16)
                r = 0
                for src, n in ((conv_w.rearrange("l t (m p) -> (l t m) p", p=P), O_CB - O_CW),
                               (conv_b.rearrange("l (m p) -> (l m) p", p=P), 2 * BC),
                               (lru_ba.rearrange("l d (m p) -> (l d m) p", p=P), 4 * BC),
                               (lru_bx.rearrange("l d (m p) -> (l d m) p", p=P), 4 * BC),
                               (lru_lambda.rearrange("l d (m p) -> (l d m) p", p=P), 4 * BC)):
                    sp.dma_start(rows_in[r:r + n, 1, :], src).then_inc(vec_in, 16)
                    r += n
                sp.dma_start(cst[:, P:], consts[:, P:]).then_inc(const_in, 16)
                sp.dma_start(rw[:, :, :], router_w[0].rearrange("(c p) e -> p c e", p=P)).then_inc(rw_in, 16)

            def mixer(l):
                if l:
                    sp.wait_ge(s_max, NA * l)
                    sp.wait_ge(lru_ps, 2 * l)
                k = 0
                for g in GROUPS:
                    for r in range(4):
                        load(BASE_MIX[l], k, square(w_in[l], r, g))
                        load_tables(l, k - 4)
                        k += 1
                        if l == 0 and k == 3:
                            load_vectors()
                for dg, b in BRANCHES:
                    for r in range(2):
                        load(BASE_MIX[l], k, square(w_branch[l, b], r, dg))
                        k += 1
                for r in range(U_OUT):
                    load(BASE_MIX[l], k, wide(w_out[l], r))
                    k += 1

            def dense():
                gu, down = ffn_w_gu[0], ffn_w_down[0]
                for r in range(4):
                    load(BASE_FF, r, square(gu, r, 0))
                for r in range(4):
                    load(BASE_FF, 4 + r, square(gu, r, FF_STEPS))
                with sp.Fori(0, FF_STEPS - 1) as i:
                    for half in range(2):
                        for r in range(4):
                            c = (i + (1 + half * FF_STEPS)) * 512
                            src = gu[256 * r:256 * r + 256, bass.ds(c, 512)].rearrange("(k p) n -> p k n", p=P)
                            load(BASE_FF + 8, 4 * half + r, src, i, 12)
                    for r in range(4):
                        src = down[bass.ds(i * 512 + r * P, P), :].rearrange("(k p) n -> p k n", p=P)
                        load(BASE_FF + 8, 8 + r, src, i, 12)
                for r in range(4):
                    load(BASE_FF, U_FF - 4 + r, wide(down, 4 * (FF_STEPS - 1) + r))

            def experts(p):
                base = BASE_MOE + p * E * U_EX
                if p == 0:
                    sp.wait_ge(lo_dve, BASE_MOE)
                    sp.wait_ge(lo_pool, BASE_MOE)
                with sp.Fori(0, E) as e:
                    k = 0
                    gu, dn = moe_w_gu[0, e], moe_w_down[0, e]
                    for what, s in (("gu", 0), ("gu", 1), ("dn", 0), ("gu", 2), ("dn", 1), ("dn", 2)):
                        if what == "gu":
                            for c in (s, FE_STEPS + s):
                                for r in range(4):
                                    load(base, k, square(gu, r, c), e, U_EX)
                                    k += 1
                        else:
                            for r in range(4):
                                load(base, k, wide(dn, 4 * s + r), e, U_EX)
                                k += 1

            sp.dma_start(h[:, 0, :], x[0, 0:P, :]).then_inc(x_in[0], 16)
            sp.dma_start(cst[:, 0:P], consts[:, 0:P]).then_inc(ident_in, 16)
            sp.dma_start(h[:, 1, :], x[0, P:2 * P, :]).then_inc(x_in[1], 16)
            mixer(0)
            dense()
            mixer(1)
            experts(0)
            sp.wait_ge(cnt_ok, 1)
            most = sp.value_load(cnt_i[0:1, 0:1], min_val=0, max_val=SEQ)
            with sp.If(most > FIRST_SLOTS):
                experts(1)
            for t in range(TT):
                sp.wait_ge(out_ok, t + 1)
                sp.dma_start(out[0, t * P:(t + 1) * P, :], hn[:, t, :]).then_inc(stored, 16)
            sp.wait_ge(stored, 16 * TT)

        @block.gpsimd
        def _(pool):
            def lo(base, k, i=0, per=0):
                u = base + k
                cut = CUT_MOE if base >= BASE_MOE else CUT
                pool.wait_ge(hi_done, i * per + (u + 1))
                pool.tensor_tensor(w_lo[:, u % RH, cut:], place(u)[0][:, cut:],
                                   w_hi[:, u % RH, cut:].bitcast(F32), ALU.subtract).then_inc(lo_pool, 1)

            def load_row(src, offset, read=None, count=0):
                if read is not None:
                    pool.wait_ge(read, count)
                pool.dma_start(row[:, :], bass.AP(src.tensor, offset, [[0, P], [1, D]])).then_inc(row_in, 16)

            def mask_tables(l, hp):
                pool.wait_ge(const_in, 16)
                pool.wait_ge(bias_in, 16 * 2 * (HEADS * l + 2 * hp + 2))
                n = 2 * BT_SLOTS
                m = cst[:, C_MASK:C_MASK + GRID_W].unsqueeze(1).to_broadcast([P, n, GRID_W])
                pool.tensor_tensor(bias_t[:, n * hp:n * hp + n, :], bias_t[:, n * hp:n * hp + n, :], m,
                                   ALU.add).then_inc(bias_ok, 1)

            def mixer(l):
                for k in range(U_MIX):
                    if k == 3:
                        load_row(b_in, l * IN_COLS + 2 * BR, normed, 2 * TT * (2 * l + 1))
                    if k in AT_MASK:
                        mask_tables(l, AT_MASK.index(k))
                    if k == 28:
                        load_row(norm_ffn_g, l * D, evac_d, evacs(DVE_EVACS, l, GROUPS.index(V)))
                    lo(BASE_MIX[l], k)

            def dense():
                for k in range(8):
                    lo(BASE_FF, k)
                load_row(norm_mix_g, D, normed, 2 * TT * 2)
                with pool.Fori(0, FF_STEPS - 1) as i:
                    for k in range(12):
                        lo(BASE_FF + 8, k, i, 12)
                for k in range(4):
                    lo(BASE_FF + U_FF - 4, k)

            def experts(p):
                with pool.Fori(0, E) as e:
                    for k in range(U_EX):
                        lo(BASE_MOE + p * E * U_EX, k, e, U_EX)

            load_row(norm_mix_g, 0)
            pool.memset(ux_t[:, :, :], 0.0).then_inc(zeroed, 1)
            mixer(0)
            dense()
            mixer(1)
            load_row(final_g, 0, normed, 2 * TT * 4)
            pool.wait_ge(hnh_ok, 1)
            pool.tensor_tensor(ylf[:, 0:D], gflat[:, 0:D], yhf[:, 0:D].bitcast(F32),
                               ALU.subtract).then_inc(hnl_pool, 1)
            experts(0)
            pool.wait_ge(cnt_ok, 1)
            most = pool.value_load(cnt_i[0:1, 0:1], min_val=0, max_val=SEQ)
            with pool.If(most > FIRST_SLOTS):
                experts(1)

        @block.scalar
        def _(act):
            links = [0]

            def link(ins):
                links[0] += 1
                ins.then_inc(act_link, 1)
                act.wait_ge(act_link, links[0])

            def hi(base, k, i=0, per=0):
                u = base + k
                ring = RAW_MOE if u >= BASE_MOE else RAW
                src, arrived, count = place(u)
                act.wait_ge(arrived, 16 * (per // ring) * i + count)
                if u >= RH:
                    act.wait_ge(unit_used, i * per + (u - RH + 1))
                act.activation(w_hi[:, u % RH, :], src, ACT.Copy).then_inc(hi_done, 1)

            def norm(n):
                if n == 0:
                    act.wait_ge(eps_ok, 1)
                link(act.activation(table_in, eps_t[:, 0:1], ACT.Sqrt))
                for t in range(TT):
                    if n == 0:
                        act.wait_ge(x_in[t], 16)
                    else:
                        act.wait_ge(h_ready, TT * (n - 1) + t + 1)
                    act.activation(junk[:, t, :], h[:, t, :], ACT.Square, accum_out=ss[:, t:t + 1]).then_inc(squares, 1)
                    act.wait_ge(squares, TT * n + t + 1)
                    act.activation(rms[:, t:t + 1], ss[:, t:t + 1], ACT.Sqrt, scale=1.0 / D,
                                   bias=eps_t[:, 0:1]).then_inc(rms_ok, 1)

            def norm_hi(n):
                for b in range(4):
                    act.wait_ge(xt_ps, 4 * n + b + 1)
                    act.activation(xhf[:, 512 * b:512 * b + 512], ps[:, 4 + b, :], ACT.Copy).then_inc(xh_ok, 1)

            def mixer(l):
                B = BASE_MIX[l]
                if l == 0:
                    norm(0)
                    hi(B, 0)
                    hi(B, 1)
                    norm_hi(0)
                    hi(B, 2)
                else:
                    for k in range(AHEAD):
                        hi(B, k)
                    norm(2 * l)
                    norm_hi(2 * l)
                for k in range(U_MIX):
                    if k + AHEAD < U_MIX:
                        hi(B, k + AHEAD)
                    if l == 0 and k == 4:
                        act.wait_ge(col_ok, 1)
                        link(act.activation(lam_w[:, 0, :], col[:, O_LAM:O_LAM + 16], ACT.Abs))
                        act.activation(lam_w[:, 1, :], lam_w[:, 0, :], ACT.Exp, scale=-1.0).then_inc(lam_act, 1)
                    if l == 0 and k == 8:
                        act.wait_ge(col2_ok, 1)
                        act.wait_ge(zeroed, 1)
                    n = k // 4 - 1
                    if k <= U_IN and k % 4 == 0 and n >= 0 and ACT_EVACS[n]:
                        g = GROUPS[n]
                        act.wait_ge(unit_used, group_end(l, n))
                        b0 = 2 * (n % 2)
                        bc = l * NB + 4 * g
                        if g == Q:
                            for m in range(2):
                                i = act.activation(q_t[:, m, :], ps[:, b0, SEQ * m:SEQ * m + SEQ], ACT.Identity,
                                                   scale=SCALE, bias=col2[:, O_BQ + 4 * l + m:O_BQ + 4 * l + m + 1])
                        elif g in (K, UX, UG):
                            for m in range(2):
                                dst = {K: k_t[:, m, :], UX: ux_t[:, m, 2:2 + SEQ],
                                       UG: ug_t[:, SEQ * m:SEQ * m + SEQ]}[g]
                                i = act.activation(dst, ps[:, b0, SEQ * m:SEQ * m + SEQ], ACT.Identity,
                                                   bias=col[:, bc + m:bc + m + 1])
                        else:
                            for m in range(4):
                                gb = col2[:, O_GB + 24 * l + 4 * (g - GATE0) + m:O_GB + 24 * l + 4 * (g - GATE0) + m + 1]
                                i = act.activation(gates[:, 4 * (g - GATE0) + m, :],
                                                   ps[:, b0 + m // 2, SEQ * (m % 2):SEQ * (m % 2) + SEQ],
                                                   ACT.Tanh, scale=0.5, bias=gb)
                        i.then_inc(evac_a, 1)
                    if k == AT_F1:
                        act.wait_ge(f1_ps, l + 1)
                        for m in range(2):
                            i = act.activation(lru[:, 0, SEQ * m:SEQ * m + SEQ], ps[:, 4 + m, 0:SEQ], ACT.Copy)
                        i.then_inc(ut_a, 1)
                    if k == AT_F2 + 1:
                        act.wait_ge(yb_full, l + 1)
                        act.activation(yhf[:, D:2 * D], lru[:, 2, :], ACT.Copy).then_inc(yb_h, 1)
                    for d, at in ((0, AT_LF), (1, AT_LB)):
                        if k == at or k == at + 1:
                            g = k - at
                            act.wait_ge(lru_ps, 2 * l + d + 1)
                            if d:
                                act.wait_ge(scanned, 2 * l + 1)
                            for m in range(BC):
                                o = (O_HBA, O_HBX)[g] + (2 * l + d) * BC + m
                                i = act.activation(lru[:, g, SEQ * m:SEQ * m + SEQ],
                                                   ps[:, 4 + 2 * g + m // 2, SEQ * (m % 2):SEQ * (m % 2) + SEQ],
                                                   ACT.Tanh, scale=0.5, bias=col2[:, o:o + 1])
                            i.then_inc(lru_tanh, 1)
                        if k == at + 2:
                            act.wait_ge(lru_tanh, 2 * (2 * l + d) + 1)
                            dst = uf_t[:, :] if d else lru[:, 2, :]
                            for m in range(BC):
                                o = (2 * l + d) * BC + m
                                i = act.activation(dst[:, SEQ * m:SEQ * m + SEQ], lru[:, 0, SEQ * m:SEQ * m + SEQ],
                                                   ACT.Tanh, scale=col2[:, O_SP + o:O_SP + o + 1],
                                                   bias=col2[:, O_SP + o:O_SP + o + 1])
                            i.then_inc(lru_dec, 1)
                        if k == at + 4:
                            act.wait_ge(lru_dec, 2 * (2 * l + d) + 1)
                            for m in range(BC):
                                o = (2 * l + d) * BC + m
                                i = act.activation(lru[:, 0, SEQ * m:SEQ * m + SEQ], lru[:, 0, SEQ * m:SEQ * m + SEQ],
                                                   ACT.Exp, scale=col2[:, O_NSP + o:O_NSP + o + 1],
                                                   bias=col2[:, O_NSP + o:O_NSP + o + 1])
                            i.then_inc(lru_dec, 1)
                        if k == at + 6:
                            dst = uf_t[:, :] if d else lru[:, 2, :]
                            act.wait_ge(mult_in, 2 * l + d + 1)
                            act.activation(dst, dst, ACT.Sqrt).then_inc(mult_ok, 1)
                    if k == AT_GELU + 2:
                        act.wait_ge(gelu_in, l + 1)
                        act.activation(lru[:, 0, :], lru[:, 0, :], ACT.Tanh, scale=GELU_C).then_inc(gelu_t, 1)
                    if k == AT_GELU + 5:
                        act.wait_ge(yc_ok, l + 1)
                        act.activation(yhf[:, 2 * D:3 * D], lru[:, 1, :], ACT.Copy, scale=0.5).then_inc(yc_h, 1)
                    j = (k - AT_ATT) // 2 if (k - AT_ATT) % 2 == 0 else -1
                    if 2 <= j < NA + 2:
                        act.wait_ge(pt_ps, NA * l + j - 1)
                        if j > 2:
                            act.wait_ge(av_ps, NA * l + j - 2)
                        act.activation(pt_t[:, :, :].rearrange("p h s -> p (h s)"), ps[:, 7, :],
                                       ACT.Copy).then_inc(pt_ok, 1)
                    if 0 <= j < NA:
                        act.wait_ge(s_max, NA * l + j + 1)
                        for hh in range(2):
                            ins = act.activation(p_t[:, j % 2, hh, :], p_t[:, j % 2, hh, :], ACT.Exp,
                                                 bias=nmax[:, j % 2, hh:hh + 1], accum_out=rsum[:, j % 2, hh:hh + 1])
                        ins.then_inc(p_exp, 1)
                    if j >= 4 and j % 2 == 0 and j - 3 < NA:
                        hp = (j - 3) // 2
                        act.wait_ge(av_ps, NA * l + j - 2)
                        act.activation(yh[:, hp, :], ps[:, 6, 0:SEQ], ACT.Copy).then_inc(ya_h, 1)
                    for dg in range(2):
                        if k == U_IN + 6 * (dg + 1) + 1:
                            for b in range(2):
                                act.wait_ge(merged, 4 * l + 2 * dg + b + 1)
                                at = 1024 * dg + 512 * b
                                act.activation(xhf[:, at:at + 512], gflat[:, at:at + 512],
                                               ACT.Copy, scale=0.5).then_inc(mh_ok, 1)

            def step_hi(n, dst, i=0, per=0):
                for b in range(2):
                    act.wait_ge(prod_ok, 2 * i * per + (2 * n - 1 + b))
                    act.activation(dst[:, 512 * b:512 * b + 512], prod_t[:, 512 * b:512 * b + 512],
                                   ACT.Copy).then_inc(ah_ok, 1)

            def dense():
                B = BASE_FF
                for k in range(AHEAD):
                    hi(B, k)
                norm(1)
                norm_hi(1)

                def silu(n, g_end, i=0):
                    act.wait_ge(unit_used, i * 12 + g_end)
                    if n > 1:
                        act.wait_ge(prod_ok, 2 * i + 2 * (n - 1))
                    for b in range(2):
                        act.activation(silu_t[:, 512 * b:512 * b + 512], ps[:, b, :], ACT.Silu).then_inc(silu_ok, 1)

                for k in range(AHEAD, 8):
                    hi(B, k)
                silu(1, B + 4)
                with act.Fori(0, FF_STEPS - 1) as i:
                    for k in range(12):
                        hi(B + 8, k, i, 12)
                        if k == 2:
                            act.wait_ge(unit_used, i * 12 + (B + 8))
                            step_hi(1, yhf[:, 0:1024], i, 1)
                        if k == 7:
                            silu(2, B + 12, i)
                for k in range(4):
                    hi(B + U_FF - 4, k)
                    if k == 0:
                        step_hi(FF_STEPS, yhf[:, 1024:2048])

            def experts(p):
                B = BASE_MOE + p * E * U_EX

                def silu(e, s):
                    act.wait_ge(unit_used, e * U_EX + (B + (4, 12, 24)[s]))
                    act.wait_ge(prod_ok, e * FE_STEPS + (ff_count(p, 0, s) - 1))
                    act.activation(silu_t[:, 0:512], ps[:, 2 * (s % 2), :], ACT.Silu).then_inc(silu_ok, 1)

                def gather_rows(n, e):
                    act.wait_ge(gr_ps, e * 2 + (2 * n + 1))
                    act.activation(xrow[:, 0:512], ps[:, 6, :], ACT.Copy).then_inc(xr_a, 1)

                def gather_hi(n, e):
                    for b in range(2):
                        act.wait_ge(gth_ps, e * 2 + (2 * n + b + 1))
                        act.activation(xg_h[:, 512 * b:512 * b + 512], ps[:, 6 + b, :], ACT.Copy).then_inc(xgh_ok, 1)

                def rows_hi(n, e):
                    act.wait_ge(unit_used, e * U_EX + (B + (E * U_EX if n % (E + 1) == 0 else 0)))
                    for b in range(2):
                        ins = act.activation(ys_h[:, 512 * b:512 * b + 512], ps[:, 4 + b, :], ACT.Copy,
                                             scale=slot_w)
                        ins.then_inc(ysh_ok, 1)

                def product_hi(e, s):
                    act.wait_ge(at_ps, e * FE_STEPS + at_count(p, s))
                    o = 2048 + 512 * (s % 2)
                    act.activation(yhf[:, o:o + 512], ps[:, 2 * (s % 2), :], ACT.Copy).then_inc(ah_ok, 1)

                if p == 0:
                    for t in range(TT):
                        act.wait_ge(normed, 2 * (TT * 3 + t + 1))
                        act.activation(yhf[:, D * t:D * t + D], gflat[:, D * t:D * t + D], ACT.Copy).then_inc(hnh_ok, 1)
                        if t == 0:
                            for b in range(2):
                                act.wait_ge(xt_ps, 4 * 3 + b + 1)
                                act.activation(xt_full[:, 512 * b:512 * b + 512], ps[:, 4 + b, :],
                                               ACT.Copy).then_inc(xt_a, 1)
                    link(act.activation(table_in, eps_t[:, 0:1], ACT.Exp))
                    for k in range(AHEAD):
                        hi(B, k)
                    act.wait_ge(lg_d, 1)
                    act.activation(wtop[:, :, 2:3], wtop[:, :, 1:2], ACT.Exp).then_inc(w2_ok, 1)
                else:
                    for k in range(AHEAD):
                        hi(B, k)
                if p == 0:
                    link(act.activation(table_in, eps_t[:, 0:1], ACT.Silu))
                gather_rows((E + 1) * p, 0)
                gather_hi((E + 1) * p, 0)
                act.wait_ge(slot_zero, p + 1)
                def turn(e, last):
                    rows_hi((E + 1) * p + 1, e)
                    for k in range(AHEAD, U_EX + AHEAD):
                        if k < U_EX or not last:
                            hi(B, k, e, U_EX)
                        if k == 4 + AHEAD:
                            silu(e, 0)
                        if k == 11 + AHEAD:
                            product_hi(e, 0)
                        if k == 12 + AHEAD:
                            silu(e, 1)
                        if k == 16 + AHEAD:
                            act.wait_ge(gt_ps, e + (E * p + 1))
                            act.activation(gt_t[:, :, :].rearrange("p t s -> p (t s)"), ps[:, 6, 0:2 * P], ACT.Copy)\
                               .then_inc(gt_ok, 1)
                            act.activation(slot_w, ps[:, 6, 2 * P:2 * P + 1], ACT.Copy).then_inc(gt_ok, 1)
                        if k == 20 + AHEAD:
                            product_hi(e, 1)
                        if k == 24 + AHEAD:
                            silu(e, 2)
                        if k == 25 + AHEAD:
                            gather_rows((E + 1) * p + 1, e)
                        if k == 28 + AHEAD:
                            gather_hi((E + 1) * p + 1, e)
                        if k == 30 + AHEAD:
                            product_hi(e, 2)

                with act.Fori(0, E - 1) as e:
                    turn(e, False)
                turn(E - 1, True)
                rows_hi((E + 1) * (p + 1), 0)

            mixer(0)
            dense()
            mixer(1)
            norm(3)
            experts(0)
            act.wait_ge(cnt_ok, 1)
            most = act.value_load(cnt_i[0:1, 0:1], min_val=0, max_val=SEQ)
            with act.If(most > FIRST_SLOTS):
                experts(1)
            norm(4)

        @block.vector
        def _(dve):
            links = [0]
            most = []

            def link(ins):
                links[0] += 1
                ins.then_inc(dve_link, 1)
                dve.wait_ge(dve_link, links[0])

            def lo(base, k, i=0, per=0):
                u = base + k
                cut = CUT_MOE if base >= BASE_MOE else CUT
                dve.wait_ge(hi_done, i * per + (u + 1))
                dve.tensor_tensor(w_lo[:, u % RH, 0:cut], place(u)[0][:, 0:cut],
                                  w_hi[:, u % RH, 0:cut].bitcast(F32), ALU.subtract).then_inc(lo_dve, 1)

            def norm(n):
                for t in range(TT):
                    dve.wait_ge(rms_ok, TT * n + t + 1)
                    link(dve.reciprocal(rinv[:, t:t + 1], rms[:, t:t + 1]))
                    if t == 0:
                        dve.wait_ge(row_in, 16 * (n + 1 + (n + 1) // 2))
                    for half in range(2):
                        q = slice(512 * half, 512 * half + 512)
                        ins = dve.scalar_tensor_tensor(out=hn[:, t, q], in0=h[:, t, q], scalar=rinv[:, t:t + 1],
                                                       in1=row[:, q], op0=ALU.mult, op1=ALU.mult)
                        if n < 4:
                            ins.then_inc(normed, 1)
                    if n == 4:
                        ins.then_inc(out_ok, 1)

            def norm_lo(n):
                for b in range(4):
                    dve.wait_ge(xh_ok, 4 * n + b + 1)
                    dve.tensor_tensor(xlf[:, 512 * b:512 * b + 512], ps[:, 4 + b, :],
                                      xhf[:, 512 * b:512 * b + 512].bitcast(F32), ALU.subtract).then_inc(xl_ok, 1)

            def add_acc(n, end):
                for t in range(TT):
                    if t == 0:
                        dve.wait_ge(acc_first, n)
                    else:
                        dve.wait_ge(unit_used, end)
                    for half in range(2):
                        ins = dve.tensor_tensor(h[:, t, 512 * half:512 * half + 512], ps[:, 4 + 2 * t + half, :],
                                                h[:, t, 512 * half:512 * half + 512], ALU.add)
                    ins.then_inc(h_ready, 1)

            def set_up_columns():
                dve.wait_ge(const_in, 16)
                dve.wait_ge(vec_t, 1)
                dve.tensor_copy(col[:, 0:2 * NB], ps[:, 4, 0:2 * NB])
                link(dve.tensor_copy(col[:, 2 * NB:N_COL], ps[:, 5, 0:N_COL - 2 * NB]))
                dve.tensor_scalar(col2[:, O_HBA:O_HBA + 32], col[:, O_BA:O_BA + 32], 0.5, None, ALU.mult)
                for l in range(2):
                    dve.tensor_scalar(col2[:, O_BQ + 4 * l:O_BQ + 4 * l + 4], col[:, l * NB + 4 * Q:l * NB + 4 * Q + 4],
                                      SCALE, None, ALU.mult)
                    dve.tensor_scalar(col2[:, O_GB + 24 * l:O_GB + 24 * l + 24],
                                      col[:, l * NB + 4 * GATE0:l * NB + 4 * GATE0 + 24], 0.5, None, ALU.mult)
                dve.tensor_scalar(lam_w[:, 5, :], col[:, O_LAM:O_LAM + 16], -1.0, 0.0, ALU.mult, ALU.max).then_inc(col_ok, 1)

            def set_up_decay():
                dve.wait_ge(lam_act, 1)
                link(dve.tensor_scalar(lam_w[:, 2, :], lam_w[:, 1, :], 2.0, None, ALU.add))
                link(dve.reciprocal(lam_w[:, 2, :], lam_w[:, 2, :]))
                link(dve.tensor_tensor(lam_w[:, 2, :], lam_w[:, 2, :], lam_w[:, 1, :], ALU.mult))
                link(dve.tensor_tensor(lam_w[:, 3, :], lam_w[:, 2, :], lam_w[:, 2, :], ALU.mult))
                link(dve.tensor_scalar(lam_w[:, 4, :], lam_w[:, 3, :], 1.0 / 19, None, ALU.mult))
                for odd in range(17, 1, -2):
                    link(dve.scalar_tensor_tensor(out=lam_w[:, 4, :], in0=lam_w[:, 4, :], scalar=1.0 / odd,
                                                  in1=lam_w[:, 3, :], op0=ALU.add, op1=ALU.mult))
                link(dve.scalar_tensor_tensor(out=lam_w[:, 4, :], in0=lam_w[:, 4, :], scalar=1.0, in1=lam_w[:, 2, :],
                                              op0=ALU.add, op1=ALU.mult))
                link(dve.scalar_tensor_tensor(out=lam_w[:, 4, :], in0=lam_w[:, 4, :], scalar=2.0, in1=lam_w[:, 5, :],
                                              op0=ALU.mult, op1=ALU.add))
                dve.tensor_scalar(col2[:, O_SP:O_SP + 16], lam_w[:, 4, :], 4.0, None, ALU.mult)
                dve.tensor_scalar(col2[:, O_NSP:O_NSP + 16], lam_w[:, 4, :], -4.0, None, ALU.mult).then_inc(col2_ok, 1)

            def mixer(l):
                B = BASE_MIX[l]
                norm(2 * l)
                if l == 0:
                    lo(B, 0)
                    lo(B, 1)
                norm_lo(2 * l)
                if l == 0:
                    lo(B, 2)
                for k in range(U_MIX):
                    if k + AHEAD < U_MIX:
                        lo(B, k + AHEAD)
                    if l == 0 and k == 4:
                        set_up_columns()
                    if l == 0 and k == 5:
                        set_up_decay()
                    n = k // 4 - 1
                    if k <= U_IN and k % 4 == 0 and n >= 0 and DVE_EVACS[n]:
                        g = GROUPS[n]
                        dve.wait_ge(unit_used, group_end(l, n))
                        b0 = 2 * (n % 2)
                        bc = l * NB + 4 * g
                        if g in (UF, V):
                            dve.wait_ge(row_in, 16 * (3 * l + 2))
                            for t in range(TT):
                                dst = uf_t[:, BR * t:BR * t + BR] if g == UF else v_t[:, t, :]
                                off = BR if g == UF else 0
                                i = dve.tensor_tensor(dst, ps[:, b0 + t, :], row[:, off:off + BR], ALU.add)
                            i.then_inc(evac_d, 1)
                        else:
                            for m in range(2, 4):
                                src = ps[:, b0 + 1, SEQ * (m - 2):SEQ * (m - 2) + SEQ]
                                if g == Q:
                                    i = dve.tensor_scalar(q_t[:, m, :], src, col[:, bc + m:bc + m + 1], SCALE,
                                                          ALU.add, ALU.mult)
                                else:
                                    dst = {K: k_t[:, m, :], UX: ux_t[:, m, 2:2 + SEQ],
                                           UG: ug_t[:, SEQ * m:SEQ * m + SEQ]}[g]
                                    if g == UX and l == 0:
                                        dve.wait_ge(zeroed, 1)
                                    i = dve.tensor_scalar(dst, src, col[:, bc + m:bc + m + 1], None, ALU.add)
                            i.then_inc(evac_d, 1)
                    if AT_CONV <= k < AT_CONV + 4:
                        tap = k - AT_CONV
                        if tap == 0:
                            dve.wait_ge(evac_a, evacs(ACT_EVACS, l, 1))
                            dve.wait_ge(evac_d, evacs(DVE_EVACS, l, 1))
                            if l:
                                dve.wait_ge(lru_ps, 2 * l)
                        for m in range(BC):
                            w = col[:, O_CW + (4 * l + tap) * BC + m:O_CW + (4 * l + tap) * BC + m + 1]
                            src = ux_t[:, m, tap:tap + SEQ]
                            if tap == 0:
                                o = O_CB + l * BC + m
                                i = dve.tensor_scalar(conv_t[:, m, :], src, w, col[:, o:o + 1], ALU.mult, ALU.add)
                            else:
                                i = dve.scalar_tensor_tensor(out=conv_t[:, m, :], in0=src, scalar=w,
                                                             in1=conv_t[:, m, :], op0=ALU.mult, op1=ALU.add)
                        if tap < 3:
                            link(i)
                        else:
                            i.then_inc(conv_ok, 1)
                    if k == AT_F1:
                        dve.wait_ge(f1_ps, l + 1)
                        for m in range(2):
                            i = dve.tensor_copy(lru[:, 0, SEQ * (2 + m):SEQ * (3 + m)], ps[:, 6 + m, 0:SEQ])
                        i.then_inc(ut_d, 1)
                    if k == AT_F2:
                        dve.wait_ge(f2_ps, l + 1)
                        for b in range(2):
                            src = ps[:, 4 + b, :].rearrange("p (m s) -> p m s", m=2)
                            dst = lru[:, 2, 512 * b:512 * b + 512].rearrange("p (m s) -> p m s", m=2)
                            dve.tensor_copy(dst[:, :, 0:P + 1], src[:, :, 0:P + 1])
                            i = dve.tensor_copy(dst[:, :, P + 1:SEQ], src[:, :, P + 1:SEQ])
                        link(i)
                        half = lru[:, 2, :].rearrange("p (m s) -> p m s", m=BC)
                        sines = lru[:, 1, :].rearrange("p (m s) -> p m s", m=BC)
                        link(dve.tensor_copy(sines[:, :, 1:P], half[:, :, P + 1:SEQ]))
                        link(dve.tensor_tensor(half[:, :, P + 1:SEQ], half[:, :, P - 1:0:-1], sines[:, :, P - 1:0:-1],
                                               ALU.subtract))
                        dve.tensor_tensor(half[:, :, 1:P], half[:, :, 1:P], sines[:, :, 1:P],
                                          ALU.add).then_inc(yb_full, 1)
                    if k == AT_F2 + 2:
                        dve.wait_ge(yb_h, l + 1)
                        dve.tensor_tensor(ylf[:, D:2 * D], lru[:, 2, :], yhf[:, D:2 * D].bitcast(F32),
                                          ALU.subtract).then_inc(yb_l, 1)
                    j = (k - AT_ATT) // 2 if (k - AT_ATT) % 2 == 0 else -1
                    if 0 <= j < NA:
                        hp, t = UNITS_ATT[j]
                        dve.wait_ge(s_ps, NA * l + j + 1)
                        dve.wait_ge(bias_ok, 4 * l + hp + 1)
                        if j >= 2:
                            dve.wait_ge(pt_ps, NA * l + j - 1)
                        s0 = 2 - 2 * t
                        bias = bias_t[:, 2 * hp * BT_SLOTS:2 * (hp + 1) * BT_SLOTS, :]\
                            .rearrange("p (h r) c -> p h r c", h=2)[:, :, s0:s0 + ROWS, ::-1]
                        b2 = j % 2
                        link(dve.tensor_tensor(p_t[:, b2, :, :].rearrange("p h (r c) -> p h r c", r=ROWS),
                                               ps[:, 4:6, 0:SEQ].rearrange("p h (r c) -> p h r c", r=ROWS), bias, ALU.add))
                        link(dve.tensor_reduce(smax[:, b2, :], p_t[:, b2, :, :], AX_X, ALU.max))
                        dve.tensor_scalar(nmax[:, b2, :], smax[:, b2, :], -1.0, None, ALU.mult).then_inc(s_max, 1)
                    if 1 <= j < NA + 1:
                        b2 = (j - 1) % 2
                        dve.wait_ge(p_exp, NA * l + j)
                        link(dve.reciprocal(rrec[:, b2, :], rsum[:, b2, :]))
                        for hh in range(2):
                            i = dve.tensor_scalar(p_t[:, b2, hh, :], p_t[:, b2, hh, :], rrec[:, b2, hh:hh + 1], None,
                                                  ALU.mult)
                        i.then_inc(p_norm, 1)
                    if j >= 4 and j % 2 == 0 and j - 3 < NA:
                        hp = (j - 3) // 2
                        dve.wait_ge(ya_h, 4 * l + hp + 1)
                        dve.tensor_tensor(yl[:, hp, :], ps[:, 6, 0:SEQ], yh[:, hp, :].bitcast(F32),
                                          ALU.subtract).then_inc(ya_l, 1)
                    for d, at in ((0, AT_LF), (1, AT_LB)):
                        t_buf = uf_t[:, :] if d else lru[:, 2, :]
                        if k == at + 5:
                            t_3d = t_buf.rearrange("p (m s) -> p m s", m=BC)
                            a_3d = lru[:, 0, :].rearrange("p (m s) -> p m s", m=BC)
                            dve.wait_ge(lru_dec, 2 * (2 * l + d) + 2)
                            link(dve.tensor_tensor(ux_in, a_3d, a_3d, ALU.mult))
                            dve.scalar_tensor_tensor(out=t_3d, in0=ux_in, scalar=1.0, in1=t_3d,
                                                     op0=ALU.add, op1=ALU.mult).then_inc(mult_in, 1)
                        if k == at + 3:
                            dve.wait_ge(lru_tanh, 2 * (2 * l + d + 1))
                            link(dve.scalar_tensor_tensor(out=lru[:, 1, :], in0=lru[:, 1, :], scalar=1.0, in1=cflat,
                                                          op0=ALU.add, op1=ALU.mult))
                        if k == at + 7:
                            first = SEQ - 1 if d else 0
                            dve.wait_ge(mult_ok, 2 * l + d + 1)
                            dve.wait_ge(lru_dec, 2 * (2 * l + d) + 2)
                            dve.memset(t_buf.rearrange("p (m s) -> p m s", m=BC)[:, :, first:first + 1], 1.0)
                            link(dve.memset(lru[:, 0, :].rearrange("p (m s) -> p m s", m=BC)[:, :, first:first + 1], 0.0))
                            link(dve.scalar_tensor_tensor(out=lru[:, 1, :], in0=t_buf, scalar=0.5, in1=lru[:, 1, :],
                                                          op0=ALU.mult, op1=ALU.mult))
                        if k == at + 8:
                            if d:
                                dve.tensor_tensor_scan(t_buf[:, ::-1], lru[:, 0, ::-1], lru[:, 1, ::-1], 0.0,
                                                       ALU.mult, ALU.add).then_inc(scanned, 1)
                            else:
                                dve.tensor_tensor_scan(t_buf, lru[:, 0, :], lru[:, 1, :], 0.0,
                                                       ALU.mult, ALU.add).then_inc(scanned, 1)
                    if k == AT_GELU + 0:
                        dve.wait_ge(scanned, 2 * l + 2)
                        dve.wait_ge(evac_a, evacs(ACT_EVACS, l, 5))
                        dve.wait_ge(evac_d, evacs(DVE_EVACS, l, 5))
                        link(dve.tensor_tensor(lru[:, 0, :], ug_t[:, :], ug_t[:, :], ALU.mult))
                        link(dve.tensor_scalar(lru[:, 0, :], lru[:, 0, :], 0.044715, 1.0, ALU.mult, ALU.add))
                    if k == AT_GELU + 1:
                        dve.tensor_tensor(lru[:, 0, :], lru[:, 0, :], ug_t[:, :], ALU.mult).then_inc(gelu_in, 1)
                    if k == AT_GELU + 2:
                        link(dve.tensor_tensor(lru[:, 2, :], lru[:, 2, :], uf_t[:, :], ALU.add))
                    if k == AT_GELU + 3:
                        link(dve.tensor_tensor(lru[:, 2, :], lru[:, 2, :], ug_t[:, :], ALU.mult))
                    if k == AT_GELU + 4:
                        dve.wait_ge(gelu_t, l + 1)
                        dve.scalar_tensor_tensor(out=lru[:, 1, :], in0=lru[:, 0, :], scalar=1.0, in1=lru[:, 2, :],
                                                 op0=ALU.add, op1=ALU.mult).then_inc(yc_ok, 1)
                    if k == AT_GELU + 7:
                        dve.wait_ge(yc_h, l + 1)
                        dve.scalar_tensor_tensor(out=ylf[:, 2 * D:3 * D], in0=lru[:, 1, :], scalar=0.5,
                                                 in1=yhf[:, 2 * D:3 * D].bitcast(F32), op0=ALU.mult,
                                                 op1=ALU.subtract).then_inc(yc_l, 1)
                    nb = (k - U_IN) // 2 - 1
                    if U_IN < k <= U_IN + U_BR and (k - U_IN) % 2 == 0:
                        dg, br = BRANCHES[nb]
                        n = len(GROUPS) + nb
                        dve.wait_ge(unit_used, group_end(l, n))
                        dve.wait_ge(evac_a, evacs(ACT_EVACS, l, n))
                        for b in range(2):
                            at = br * 2048 + 1024 * dg + 512 * b
                            i = dve.scalar_tensor_tensor(out=gflat[:, at:at + 512], in0=gflat[:, at:at + 512],
                                                         scalar=1.0, in1=ps[:, 2 * (n % 2) + b, :],
                                                         op0=ALU.add, op1=ALU.mult)
                        i.then_inc(evac_d, 1)
                        if nb % 3 == 2:
                            dve.wait_ge(evac_d, evacs(DVE_EVACS, l, n))
                            for b in range(2):
                                at = 1024 * dg + 512 * b
                                i = dve.tensor_tensor(gflat[:, 2048 + at:2048 + at + 512], gflat[:, 2048 + at:2048 + at + 512],
                                                      gflat[:, 4096 + at:4096 + at + 512], ALU.add)
                            link(i)
                            for b in range(2):
                                at = 1024 * dg + 512 * b
                                dve.tensor_tensor(gflat[:, at:at + 512], gflat[:, at:at + 512],
                                                  gflat[:, 2048 + at:2048 + at + 512], ALU.add).then_inc(merged, 1)
                    for dg in range(2):
                        if k == U_IN + 6 * (dg + 1) + 1:
                            for b in range(2):
                                dve.wait_ge(mh_ok, 4 * l + 2 * dg + b + 1)
                                at = 1024 * dg + 512 * b
                                dve.scalar_tensor_tensor(out=xlf[:, at:at + 512], in0=gflat[:, at:at + 512], scalar=0.5,
                                                         in1=xhf[:, at:at + 512].bitcast(F32), op0=ALU.mult,
                                                         op1=ALU.subtract).then_inc(ml_ok, 1)
                if l == 0:
                    for k in range(AHEAD):
                        lo(BASE_FF, k)
                add_acc(2 * l + 1, B + U_MIX)

            def product(n, b_u, u_end, i=0, per=0, units=0):
                dve.wait_ge(unit_used, i * units + u_end)
                if n > 1:
                    dve.wait_ge(al_ok, 2 * i * per + 2 * (n - 1))
                for b in range(2):
                    dve.wait_ge(silu_ok, 2 * i * per + (2 * n - 1 + b))
                    dve.tensor_tensor(prod_t[:, 512 * b:512 * b + 512], ps[:, b_u + b, :],
                                      silu_t[:, 512 * b:512 * b + 512], ALU.mult).then_inc(prod_ok, 1)

            def step_lo(n, i=0, per=0, at=0):
                for b in range(2):
                    dst = slice(at + 512 * b, at + 512 * b + 512)
                    dve.wait_ge(ah_ok, 2 * i * per + (2 * n - 1 + b))
                    dve.tensor_tensor(ylf[:, dst], prod_t[:, 512 * b:512 * b + 512], yhf[:, dst].bitcast(F32),
                                      ALU.subtract).then_inc(al_ok, 1)

            def dense():
                B = BASE_FF
                norm(1)
                norm_lo(1)
                for k in range(AHEAD, 8):
                    lo(B, k)
                with dve.Fori(0, FF_STEPS - 1) as i:
                    for k in range(12):
                        lo(B + 8, k, i, 12)
                        if k == 0:
                            product(1, 2, B + 8, i, 1, 12)
                        if k == 3:
                            step_lo(1, i, 1)
                for k in range(4):
                    lo(B + U_FF - 4, k)
                    if k == 0:
                        product(FF_STEPS, 2, B + U_FF - 8)
                        step_lo(FF_STEPS, at=1024)
                for k in range(AHEAD):
                    lo(BASE_MIX[1], k)
                add_acc(2, B + U_FF)

            def build_g(p, e):
                for t in range(TT):
                    ins = dve.tensor_scalar(g_t[:, t, :], cst[:, C_IOTA + P * p:C_IOTA + P * p + P],
                                            pos[:, t, bass.ds(e, 1)], mask[:, t, bass.ds(e, 1)],
                                            ALU.is_equal, ALU.mult)
                ins.then_inc(g_ok, 1)

            def experts(p):
                B = BASE_MOE + p * E * U_EX

                def product_rows(s, e):
                    dve.wait_ge(unit_used, e * U_EX + (B + (8, 16, 28)[s]))
                    dve.wait_ge(silu_ok, e * FE_STEPS + ff_count(p, 0, s))
                    dve.wait_ge(prod_ok, e * FE_STEPS + (ff_count(p, 0, s) - 1))
                    if s or p:
                        dve.wait_ge(at_ps, e * FE_STEPS + (at_count(p, s) - 1))
                    dve.tensor_tensor(prod_t[:, 0:512], ps[:, 2 * (s % 2) + 1, :], silu_t[:, 0:512],
                                      ALU.mult).then_inc(prod_ok, 1)

                def product_lo(s, e):
                    dve.wait_ge(ah_ok, e * FE_STEPS + ff_count(p, 0, s))
                    o = 2048 + 512 * (s % 2)
                    dve.tensor_tensor(ylf[:, o:o + 512], ps[:, 2 * (s % 2), :], yhf[:, o:o + 512].bitcast(F32),
                                      ALU.subtract).then_inc(al_ok, 1)

                def gather_rows(n, e):
                    dve.wait_ge(gr_ps, e * 2 + (2 * n + 2))
                    dve.tensor_copy(xrow[:, 512:1024], ps[:, 7, :]).then_inc(xr_d, 1)

                def gather_lo(n, e):
                    for b in range(2):
                        dve.wait_ge(xgh_ok, e * 2 + (2 * n + b + 1))
                        dve.tensor_tensor(xg_l[:, 512 * b:512 * b + 512], ps[:, 6 + b, :],
                                          xg_h[:, 512 * b:512 * b + 512].bitcast(F32), ALU.subtract).then_inc(xgl_ok, 1)

                def rows_lo(n, e):
                    for b in range(2):
                        dve.wait_ge(ysh_ok, e * 2 + (2 * (n - 1) + b + 1))
                        dve.scalar_tensor_tensor(out=ys_l[:, 512 * b:512 * b + 512], in0=ps[:, 4 + b, :], scalar=slot_w,
                                                 in1=ys_h[:, 512 * b:512 * b + 512].bitcast(F32), op0=ALU.mult,
                                                 op1=ALU.subtract).then_inc(ysl_ok, 1)

                def scatter_add(n, e, qs=range(4)):
                    for q in qs:
                        t, half = q // 2, q % 2
                        dve.wait_ge(sc_ps, e * 4 + (4 * (n - 1) + q + 1))
                        dve.tensor_tensor(h[:, t, 512 * half:512 * half + 512], ps[:, (6, 7, 4, 5)[q], :],
                                          h[:, t, 512 * half:512 * half + 512], ALU.add).then_inc(sc_add, 1)

                if p == 0:
                    for b in range(2):
                        dve.wait_ge(xt_ps, 4 * 3 + 2 + b + 1)
                        dve.tensor_copy(xt_full[:, 1024 + 512 * b:1024 + 512 * b + 512], ps[:, 6 + b, :])\
                            .then_inc(xt_d, 1)
                    link(dve.memset(gt_t[:, :, :].bitcast(F32), 0.0))
                    dve.wait_ge(hnh_ok, 2)
                    dve.tensor_tensor(ylf[:, D:2 * D], gflat[:, D:2 * D], yhf[:, D:2 * D].bitcast(F32),
                                      ALU.subtract).then_inc(hnl_dve, 1)
                    lo(B, 0)
                    route()
                build_g(p, 0)
                if p == 0:
                    route_weights()
                dve.memset(slot_w, 0.0).then_inc(slot_zero, 1)
                for k in range(1 if p == 0 else 0, AHEAD):
                    lo(B, k)
                gather_rows((E + 1) * p, 0)
                gather_lo((E + 1) * p, 0)
                def turn(e, last):
                    rows_lo((E + 1) * p + 1, e)
                    for k in range(AHEAD, U_EX + AHEAD):
                        if k == 31:
                            product_rows(2, e)
                        if k < U_EX or not last:
                            lo(B, k, e, U_EX)
                        if last and p == 0 and k == 5:
                            most.append(dve.value_load(cnt_i[0:1, 0:1], min_val=0, max_val=SEQ))
                        if k == 11:
                            product_rows(0, e)
                        if k in (12, 13):
                            scatter_add((E + 1) * p + 1, e, (range(0, 2), range(2, 4))[k - 12])
                        if k == 14:
                            product_lo(0, e)
                        if k == 19:
                            product_rows(1, e)
                        if k == 23:
                            dve.wait_ge(gt_ps, e + (E * p + 1))
                            build_g(p, e + 1)
                            product_lo(1, e)
                        if k == 28:
                            gather_rows((E + 1) * p + 1, e)
                        if k == 31:
                            gather_lo((E + 1) * p + 1, e)
                        if k == 33:
                            product_lo(2, e)

                with dve.Fori(0, E - 1) as e:
                    turn(e, False)
                turn(E - 1, True)
                rows_lo((E + 1) * (p + 1), 0)
                scatter_add((E + 1) * (p + 1), 0)
                dve.wait_ge(sc_add, 4 * (E + 1) * (p + 1))

            def route():
                link(dve.memset(small[:, 80:152], 0.0))
                dve.wait_ge(lg_ps, 1)
                dve.tensor_copy(p_t[0:E, 0, 0, :], ps[0:E, 0, 0:SEQ]).then_inc(lg_row, 1)
                dve.wait_ge(lg_t, 1)
                link(dve.tensor_copy(logit, ps[:, 1, 0:TT * E].rearrange("p (t e) -> p t e", t=TT)))
                for t in range(TT):
                    i = dve.max(top8[:, t, :], logit[:, t, :])
                link(i)
                for t in range(TT):
                    i = dve.max_index(idx[:, t, :], top8[:, t, :], logit[:, t, :])
                link(i)
                link(dve.tensor_copy(idxf[:, :, 0:2], idx[:, :, 0:2]))
                for t in range(TT):
                    for j, oh in enumerate((oh1, oh2)):
                        i = dve.tensor_scalar(oh[:, t, :], cst[:, C_I8:C_I8 + E], idxf[:, t, j:j + 1], None,
                                              ALU.is_equal)
                link(i)
                dve.tensor_tensor(mask[:, :, 0:E], oh1, oh2, ALU.add).then_inc(mask_ok, 1)
                dve.tensor_tensor(wtop[:, :, 1:2], top8[:, :, 1:2], top8[:, :, 0:1], ALU.subtract).then_inc(lg_d, 1)
                dve.wait_ge(pos_ps, 1)
                link(dve.tensor_copy(pos[:, :, 0:E], ps[:, 1, 64:64 + TT * E].rearrange("p (t e) -> p t e", t=TT)))

            def route_weights():
                dve.wait_ge(w2_ok, 1)
                link(dve.tensor_scalar(wtop[:, :, 3:4], wtop[:, :, 2:3], 1.0, None, ALU.add))
                link(dve.reciprocal(wtop[:, :, 4:5], wtop[:, :, 3:4]))
                link(dve.tensor_tensor(wtop[:, :, 5:6], wtop[:, :, 4:5], wtop[:, :, 2:3], ALU.mult))
                for t in range(TT):
                    i = dve.tensor_scalar(comb[:, t, 0:E], oh1[:, t, :], wtop[:, t, 4:5], None, ALU.mult)
                link(i)
                for t in range(TT):
                    i = dve.scalar_tensor_tensor(out=comb[:, t, 0:E], in0=oh2[:, t, :], scalar=wtop[:, t, 5:6],
                                                 in1=comb[:, t, 0:E], op0=ALU.mult, op1=ALU.add)
                i.then_inc(comb_ok, 1)
                dve.wait_ge(cnt_ps, 1)
                link(dve.tensor_reduce(cmax, ps[:, 3, 0:E], AX_X, ALU.max))
                dve.tensor_copy(cnt_i[:, 0:1], cmax).then_inc(cnt_ok, 1)
                dve.wait_ge(cnt_ok, 1)

            dve.memset(eps_t[:, :], EPS).then_inc(eps_ok, 1)
            mixer(0)
            dense()
            mixer(1)
            norm(3)
            experts(0)
            with dve.If(most[0] > FIRST_SLOTS):
                experts(1)
            dve.memset(cmax, 0.0).then_inc(h_ready, TT)
            norm(4)

        @block.tensor
        def _(pe):
            mm = pe.matmul

            def mm3(dst, ah, al, bh, bl, first, last):
                mm(dst, ah, bh, start=first, stop=False, skip_group_check=True)
                mm(dst, ah, bl, start=False, stop=False, skip_group_check=True)
                return mm(dst, al, bh, start=False, stop=last, skip_group_check=True)

            def split(base, k, i=0, per=0):
                u = base + k
                pe.wait_ge(lo_dve, i * per + (u + 1))
                pe.wait_ge(lo_pool, i * per + (u + 1))
                return w_hi[:, u % RH, :], w_lo[:, u % RH, :]

            def unit_columns(base, k, r, banks, xs, width, i=0, per=0, last=None):
                wh, wl = split(base, k, i, per)
                for kk in range(2):
                    for m in range(4):
                        at = width * m
                        dst = ps[:, banks + at // 512, at % 512:at % 512 + width]
                        c = 2 * r + kk
                        o = 512 * kk + P * m
                        ins = mm3(dst, wh[:, o:o + P], wl[:, o:o + P], xs[0][:, width * c:width * c + width],
                                  xs[1][:, width * c:width * c + width],
                                  first=(c == 0 and at % 512 == 0), last=(last == c))
                ins.then_inc(unit_used, 1)
                return ins

            def unit_tokens(base, k, r, banks, i=0, per=0):
                wh, wl = split(base, k, i, per)
                for kk in range(2):
                    for t in range(TT):
                        c = 2 * r + kk
                        ins = mm3(ps[:, banks + t, :], xh[:, c, P * t:P * t + P], xl[:, c, P * t:P * t + P],
                                  wh[:, 512 * kk:512 * kk + 512], wl[:, 512 * kk:512 * kk + 512],
                                  first=(c == 0), last=(c == KC - 1))
                ins.then_inc(unit_used, 1)

            def unit_wide(base, k, a_h, a_l, tiles, first, last, i=0, per=0):
                wh, wl = split(base, k, i, per)
                for t in range(tiles):
                    for half in range(2):
                        ins = mm3(ps[:, 4 + 2 * t + half, :], a_h[:, P * t:P * t + P], a_l[:, P * t:P * t + P],
                                  wh[:, 512 * half:512 * half + 512], wl[:, 512 * half:512 * half + 512],
                                  first=first, last=last)
                    if last and t < tiles - 1:
                        ins.then_inc(acc_first, 1)
                ins.then_inc(unit_used, 1)

            def keep_warm(n):
                for _ in range(n):
                    pe.transpose(ps[:, 2, 0:P], ident, ident)

            def norm(n):
                for t in range(TT):
                    if n == 0:
                        keep_warm((8, 6)[t])
                    for c in range(KC):
                        if c % (KC // 2) == 0:
                            pe.wait_ge(normed, 2 * (TT * n + t) + c // (KC // 2) + 1)
                        at = SEQ * (c % 2) + P * t
                        ins = pe.transpose(ps[:, 4 + c // 2, at:at + P], hn[:, t, P * c:P * c + P], ident)
                        if t == TT - 1 and c % 2:
                            ins.then_inc(xt_ps, 1)

            def mixer(l):
                B = BASE_MIX[l]
                norm(2 * l)
                if l == 0:
                    keep_warm(6)
                for k in range(U_MIX):
                    if l == 0 and k == 4:
                        pe.wait_ge(vec_in, 16 * 6)
                        pe.transpose(ps[:, 4, 0:2 * NB], rows_in[0:2 * NB, 0, :], ident[0:2 * NB, 0:2 * NB])
                        n = N_COL - 2 * NB
                        pe.transpose(ps[:, 5, 0:n], rows_in[0:n, 1, :], ident[0:n, 0:n]).then_inc(vec_t, 1)
                    if l == 0 and k == AT_F1:
                        pe.wait_ge(col_ok, 1)
                        pe.wait_ge(const_in, 16)
                    if k == AT_F1:
                        pe.wait_ge(evac_d, evacs(DVE_EVACS, l, 0))
                        pe.wait_ge(xl_ok, 8 * l + 4)
                        for m in range(BC):
                            for t in range(TT):
                                at = C_DFT + SEQ * t
                                ins = mm(ps[:, 4 + m, 0:SEQ], uf_t[:, BR * t + P * m:BR * t + P * m + P],
                                         cst[:, at:at + SEQ], start=(t == 0), stop=(t == TT - 1))
                        ins.then_inc(f1_ps, 1)
                    if k == AT_F2:
                        pe.wait_ge(ut_a, l + 1)
                        pe.wait_ge(ut_d, l + 1)
                        for m in range(BC):
                            for s, (c0, c1) in enumerate(((0, P + 1), (P + 1, SEQ))):
                                ins = mm(ps[:, 4 + m // 2, SEQ * (m % 2) + c0:SEQ * (m % 2) + c1],
                                         cst[:, C_CC + P * s:C_CC + P * s + P], lru[:, 0, SEQ * m + c0:SEQ * m + c1],
                                         start=True, stop=True)
                        ins.then_inc(f2_ps, 1)
                    for d, at in ((0, AT_LF), (1, AT_LB)):
                        if k == at:
                            if d:
                                pe.wait_ge(lru_tanh, 2 * (2 * l + 1))
                            else:
                                pe.wait_ge(yb_l, l + 1)
                                pe.wait_ge(conv_ok, l + 1)
                                pe.wait_ge(wlru_in, 16 * 8 * (l + 1))
                            for g in range(2):
                                for m in range(BC):
                                    for hh in range(2):
                                        q = slice(HD * hh, HD * hh + HD)
                                        ins = mm(ps[q, 4 + 2 * g + m // 2, SEQ * (m % 2):SEQ * (m % 2) + SEQ],
                                                 wlru[q, d, g, m, :], conv_t[q, m, :], start=True, stop=True)
                            ins.then_inc(lru_ps, 1)
                    j = (k - AT_ATT) // 2 if (k - AT_ATT) % 2 == 0 else -1
                    if 0 <= j < NA:
                        hp, t = UNITS_ATT[j]
                        if j == 0:
                            pe.wait_ge(evac_a, evacs(ACT_EVACS, l, 3))
                            pe.wait_ge(evac_d, evacs(DVE_EVACS, l, 4))
                            pe.wait_ge(lru_tanh, 4 * (l + 1))
                        else:
                            pe.wait_ge(s_max, NA * l + j)
                        for hh in range(2):
                            q = slice(HD * hh, HD * hh + HD)
                            ins = mm(ps[:, 4 + hh, 0:SEQ], q_t[q, hp, P * t:P * t + P], k_t[q, hp, :],
                                     start=True, stop=True)
                        ins.then_inc(s_ps, 1)
                    if 3 <= j < NA + 3:
                        hp, t = UNITS_ATT[j - 3]
                        pe.wait_ge(pt_ok, NA * l + j - 2)
                        if hp >= 1 and t == 0:
                            pe.wait_ge(ya_l, 4 * l + hp)
                        for kt in range(TT):
                            for hh in range(2):
                                hd = 2 * hp + hh
                                ins = mm(ps[HD * hh:HD * hh + HD, 6, P * t:P * t + P],
                                         v_t[:, kt, HD * hd:HD * hd + HD], pt_t[:, hh, P * kt:P * kt + P],
                                         start=(kt == 0), stop=(kt == TT - 1))
                        ins.then_inc(av_ps, 1)
                    if 2 <= j < NA + 2:
                        pe.wait_ge(p_norm, NA * l + j - 1)
                        if j > 2:
                            pe.wait_ge(pt_ok, NA * l + j - 2)
                        for hh in range(2):
                            for kt in range(TT):
                                at = SEQ * hh + P * kt
                                ins = pe.transpose(ps[:, 7, at:at + P], p_t[:, j % 2, hh, P * kt:P * kt + P], ident)
                        ins.then_inc(pt_ps, 1)
                    if k < U_IN:
                        n, r = k // 4, k % 4
                        if r == 0:
                            if n >= 2:
                                pe.wait_ge(evac_a, evacs(ACT_EVACS, l, n - 2))
                                pe.wait_ge(evac_d, evacs(DVE_EVACS, l, n - 2))
                            elif l and n == 0:
                                pe.wait_ge(prod_ok, 2 * FF_STEPS)
                        if n == 0:
                            pe.wait_ge(xl_ok, 8 * l + r + 1)
                        if GROUPS[n] in (UF, V):
                            unit_tokens(B, k, r, 2 * (n % 2))
                        else:
                            unit_columns(B, k, r, 2 * (n % 2), (xhf, xlf), SEQ, last=KC - 1)
                    elif k < U_IN + U_BR:
                        nb, r = (k - U_IN) // 2, (k - U_IN) % 2
                        dg, br = BRANCHES[nb]
                        n = len(GROUPS) + nb
                        if r == 0:
                            pe.wait_ge(evac_a, evacs(ACT_EVACS, l, n - 2))
                            pe.wait_ge(evac_d, evacs(DVE_EVACS, l, n - 2))
                            if dg == 0:
                                y_ok, count = ((ya_l, 4 * l + 4), (yb_l, l + 1), (yc_l, l + 1))[br]
                                pe.wait_ge(y_ok, count)
                        unit_columns(B, k, r, 2 * (n % 2), (yhf[:, 1024 * br:1024 * br + 1024], ylf[:, 1024 * br:1024 * br + 1024]),
                                     SEQ, last=BC - 1)
                    else:
                        r = k - U_IN - U_BR
                        if r % 2 == 0:
                            pe.wait_ge(ml_ok, 4 * l + r // 2 + 1)
                        unit_wide(B, k, xh[:, r, :], xl[:, r, :], TT, r == 0, r == U_OUT - 1)

            def dense():
                B = BASE_FF
                norm(1)

                def gate_up(B, n, i=0, per=0):
                    for k in range(8):
                        if k < 4 and n == 1:
                            pe.wait_ge(xl_ok, 4 + k + 1)
                        if n > 1 and k == 0:
                            pe.wait_ge(silu_ok, 2 * i + 2 * (n - 1))
                        if n > 1 and k == 4:
                            pe.wait_ge(prod_ok, 2 * i + 2 * (n - 1))
                        unit_columns(B, k, k % 4, 2 * (k // 4), (xhf, xlf), SEQ, i, per, last=KC - 1)

                def down(B, n, first, last, i=0, per=0, c=0):
                    for k in range(4):
                        if k % 2 == 0:
                            pe.wait_ge(al_ok, 2 * i + (2 * n - 1 + k // 2))
                        unit_wide(B, k, yh[:, c + k, :], yl[:, c + k, :], TT, first and k == 0, last and k == 3, i, per)

                gate_up(B, 1)
                gate_up(B + 8, 2)
                down(B + 16, 1, True, False)
                with pe.Fori(0, FF_STEPS - 2) as i:
                    gate_up(B + 20, 3, i, 12)
                    down(B + 28, 2, False, False, i, 12)
                down(B + U_FF - 4, FF_STEPS, False, True, c=BC)

            def gather(n, e):
                pe.wait_ge(g_ok, e + n)
                for half in range(2):
                    for t in range(TT):
                        o = D * t + 512 * half
                        mm(ps[:, 6 + half, :], g_t[:, t, :], yhf[:, o:o + 512], start=(t == 0), stop=False)
                        ins = mm(ps[:, 6 + half, :], g_t[:, t, :], ylf[:, o:o + 512], start=False, stop=(t == TT - 1))
                    ins.then_inc(gr_ps, 1)

            def turn_rows(n, e):
                for c in range(KC):
                    if c == 0:
                        pe.wait_ge(xr_a, e + n)
                    if c == KC // 2:
                        pe.wait_ge(xr_d, e + n)
                    ins = pe.transpose(ps[:, 6 + c // 4, P * (c % 4):P * (c % 4) + P], xrow[:, P * c:P * c + P], ident)
                    if c % 4 == 3:
                        ins.then_inc(gth_ps, 1)

            def scatter(n, e):
                pe.wait_ge(ysl_ok, e * 2 + 2 * n)
                for q in range(4):
                    t, half = q // 2, q % 2
                    dst = ps[:, (6, 7, 4, 5)[q], :]
                    mm(dst, gt_t[:, t, :], ys_h[:, 512 * half:512 * half + 512], start=True, stop=False)
                    mm(dst, gt_t[:, t, :], ys_l[:, 512 * half:512 * half + 512], start=False,
                       stop=True).then_inc(sc_ps, 1)

            def route():
                pe.wait_ge(rw_in, 16)
                for c in range(KC):
                    if c % 2 == 0:
                        pe.wait_ge(xt_a if c < KC // 2 else xt_d, (c % (KC // 2)) // 2 + 1)
                    ins = mm(ps[0:E, 0, 0:SEQ], rw[:, c, :], xt_full[:, SEQ * c:SEQ * c + SEQ],
                             start=(c == 0), stop=(c == KC - 1))
                ins.then_inc(lg_ps, 1)
                keep_warm(4)
                pe.wait_ge(lg_row, 1)
                for t in range(TT):
                    ins = pe.transpose(ps[:, 1, E * t:E * t + E], p_t[0:E, 0, 0, P * t:P * t + P], ident[0:E, 0:E])
                ins.then_inc(lg_t, 1)
                keep_warm(16)
                pe.wait_ge(mask_ok, 1)
                mm(ps[:, 1, 64:64 + E], tri, mask[:, 0, 0:E], start=True, stop=True)
                mm(ps[:, 1, 64 + E:64 + 2 * E], tri, mask[:, 1, 0:E], start=True, stop=False)
                mm(ps[:, 1, 64 + E:64 + 2 * E], ones, mask[:, 0, 0:E], start=False, stop=True).then_inc(pos_ps, 1)
                mm(ps[:, 3, 0:E], ones, mask[:, 0, 0:E], start=True, stop=False)
                mm(ps[:, 3, 0:E], ones, mask[:, 1, 0:E], start=False, stop=True).then_inc(cnt_ps, 1)

            def experts(p):
                B = BASE_MOE + p * E * U_EX
                n0 = (E + 1) * p
                if p == 0:
                    pe.wait_ge(hnl_dve, 1)
                    pe.wait_ge(hnl_pool, 1)
                    keep_warm(5)
                gather(n0 + 1, 0)
                if p == 0:
                    keep_warm(3)
                turn_rows(n0 + 1, 0)
                if p == 0:
                    keep_warm(6)
                pe.wait_ge(comb_ok, 1)
                pe.wait_ge(cnt_ok, 1)

                def gate_up(k0, s, e, ks=range(8)):
                    for k in ks:
                        if s == 0 and k == 0:
                            pe.wait_ge(prod_ok, e * FE_STEPS + (ff_count(p, 0, 0) - 1))
                        if s == 0 and k in (0, 2):
                            pe.wait_ge(xgl_ok, e * 2 + (2 * n0 + 1 + k // 2))
                        if s == 2 and k == 0:
                            pe.wait_ge(prod_ok, e * FE_STEPS + ff_count(p, 0, 0))
                        wh, wl = split(B, k0 + k, e, U_EX)
                        for kk in range(2):
                            c = 2 * (k % 4) + kk
                            ins = mm3(ps[:, 2 * (s % 2) + k // 4, :], xg_h[:, P * c:P * c + P], xg_l[:, P * c:P * c + P],
                                      wh[:, 512 * kk:512 * kk + 512], wl[:, 512 * kk:512 * kk + 512],
                                      first=(c == 0), last=(c == KC - 1))
                        ins.then_inc(unit_used, 1)

                def turn_product(s, e):
                    pe.wait_ge(prod_ok, e * FE_STEPS + ff_count(p, 0, s))
                    for m in range(4):
                        ins = pe.transpose(ps[:, 2 * (s % 2), P * m:P * m + P], prod_t[:, P * m:P * m + P], ident)
                    ins.then_inc(at_ps, 1)

                def down(k0, s, e, ks=range(4)):
                    pe.wait_ge(al_ok, e * FE_STEPS + ff_count(p, 0, s))
                    if s == 0:
                        pe.wait_ge(ysl_ok, e * 2 + 2 * (n0 + 1))
                    for k in ks:
                        o = 2048 + 512 * (s % 2) + P * k
                        unit_wide(B, k0 + k, yhf[:, o:o + P], ylf[:, o:o + P], 1, s == 0 and k == 0,
                                  s == FE_STEPS - 1 and k == 3, e, U_EX)

                with pe.Fori(0, E) as e:
                    gate_up(0, 0, e)
                    scatter(n0 + 1, e)
                    gate_up(8, 1, e, range(3))
                    turn_product(0, e)
                    gate_up(8, 1, e, range(3, 8))
                    pe.wait_ge(sc_add, e * 4 + 4 * (n0 + 1))
                    for t in range(TT):
                        pe.transpose(ps[:, 6, P * t:P * t + P], g_t[:, t, :].bitcast(F32), ident)
                    for t in range(TT):
                        ins = mm(ps[:, 6, 2 * P:2 * P + 1], g_t[:, t, :].bitcast(F32), comb[:, t, bass.ds(e, 1)],
                                 start=(t == 0), stop=(t == TT - 1))
                    ins.then_inc(gt_ps, 1)
                    down(16, 0, e)
                    turn_product(1, e)
                    gate_up(20, 2, e, range(5))
                    pe.wait_ge(gt_ok, e * 2 + 2 * (E * p + 1))
                    gather(n0 + 2, e)
                    gate_up(20, 2, e, range(5, 8))
                    turn_rows(n0 + 2, e)
                    down(28, 1, e, range(2))
                    turn_product(2, e)
                    down(28, 1, e, range(2, 4))
                    down(32, 2, e)
                scatter(n0 + E + 1, 0)

            pe.wait_ge(ident_in, 16)
            mixer(0)
            dense()
            mixer(1)
            norm(3)
            route()
            experts(0)
            pe.wait_ge(cnt_ok, 1)
            most = pe.value_load(cnt_i[0:1, 0:1], min_val=0, max_val=SEQ)
            with pe.If(most > FIRST_SLOTS):
                experts(1)


_INS = ["x", "norm_mix_g", "w_in", "b_in", "na_rpb", "conv_w", "conv_b", "lru_wa", "lru_ba", "lru_wx", "lru_bx",
        "lru_lambda", "w_branch", "w_out", "norm_ffn_g", "ffn_w_gu", "ffn_w_down", "router_w", "moe_w_gu",
        "moe_w_down", "final_g"]


def kernel(**inputs):
    import concourse.bacc as _bacc
    from concourse.bass_utils import run_bass_kernel_spmd as _run

    arrays = {name: np.asarray(inputs[name]) for name in _INS}
    rpb = np.zeros(arrays["na_rpb"].shape[:3] + (P,), np.float32)
    rpb[..., GRID_W - KW:GRID_W + KW - 1] = arrays["na_rpb"][..., ::-1]
    arrays["na_rpb"] = rpb
    arrays["consts"] = constants()
    nc = _bacc.Bacc("TRN2", target_bir_lowering=False, num_devices=1)
    feeds, args = {}, []
    for name, a in arrays.items():
        a = np.ascontiguousarray(a)
        feeds[f"in_{name}_dram"] = a
        args.append(nc.dram_tensor(f"in_{name}_dram", a.shape, mybir.dt.from_np(a.dtype), kind="ExternalInput").ap())
    args.append(nc.dram_tensor("out_0_dram", (1, SEQ, D), F32, kind="ExternalOutput").ap())
    build(nc, *args)
    r = _run(nc, [feeds], core_ids=[0])
    return r.results[0]["out_0_dram"]
```
